# Optimizing a Trainium2 kernel written in Bass

```python
import math
import jax, jax.numpy as jnp
from jax import lax
import numpy as np

D_MODEL = 1024
BATCH = 1
SEQ = 256
DEPTH = 2
DEC_BATCH = 8
DEC_SEQ = 1
PAST_LEN = 2048
PAGE_SIZE = 128

EPS = 1e-6
A_GROUPS = ((128, 1), (512, 4), (2048, 16))
N_GROUPS = 3
A_HEADS = 8
A_DH = 64
A_WIDTH = A_HEADS * A_DH
N_BUCKETS = 32
MAX_DIST = 2048
B_HEADS = 4
B_DK = 64
B_DV = 128
B_RANK = 16
B_TAU = 16.0
B_CHUNK = 64
C_HEADS = 4
C_DK = 128
C_DV = 128
CONV_W = 4
C_CONV_CH = 2 * C_HEADS * C_DK + C_HEADS * C_DV
C_CHUNK = 64
BRANCH_W = 512
D_FF = 2816
N_EXPERTS = 8
TOP_K = 2
D_FF_EXPERT = 1792
N_DENSE = (DEPTH + 1) // 2
N_MOE = DEPTH // 2
IN_SIZES = (N_GROUPS * A_WIDTH, N_GROUPS * A_WIDTH, N_GROUPS * A_WIDTH,
            B_HEADS * B_DK, B_HEADS * B_DK, B_HEADS * B_DV, B_HEADS * B_DV, B_RANK,
            C_CONV_CH, C_HEADS * C_DV, C_HEADS, C_HEADS, 3 * D_MODEL)
N_IN = sum(IN_SIZES)

kernel_name = 'hybrid_dilated_gla_gdn_decode_step'

def split_points():
    pts, acc = [], 0
    for s in IN_SIZES[:-1]:
        acc += s
        pts.append(acc)
    return pts

def rms_norm(x, w):
    xf = x.astype(jnp.float32)
    y = xf * lax.rsqrt(jnp.mean(xf * xf, axis=-1, keepdims=True) + EPS)
    return (y * w.astype(jnp.float32)).astype(x.dtype)

def l2_norm(x):
    xf = x.astype(jnp.float32)
    return (xf * lax.rsqrt(jnp.sum(xf * xf, axis=-1, keepdims=True) + EPS)).astype(x.dtype)

def t5_bucket(dist):
    max_exact = N_BUCKETS // 2
    d = jnp.maximum(dist.astype(jnp.float32), 1.0)
    large = max_exact + (jnp.log(d / max_exact) / math.log(MAX_DIST / max_exact)
                         * (N_BUCKETS - max_exact)).astype(jnp.int32)
    large = jnp.minimum(large, N_BUCKETS - 1)
    return jnp.where(dist < max_exact, dist, large).astype(jnp.int32)

def dilated_prompt(q, k, v, bias_g, window, dil):
    B, S, H, Dh = q.shape
    span = window // dil
    L = S // dil
    nb = -(-L // span)
    pad_back = nb * span - L

    def by_residue(t):
        return t.reshape(B, L, dil, H, Dh).transpose(0, 2, 1, 3, 4)

    qb = jnp.pad(by_residue(q), ((0, 0), (0, 0), (0, pad_back), (0, 0), (0, 0))).reshape(B, dil, nb, span, H, Dh)

    def key_blocks(t):
        tp = jnp.pad(by_residue(t), ((0, 0), (0, 0), (span, pad_back), (0, 0), (0, 0)))
        tp = tp.reshape(B, dil, nb + 1, span, H, Dh)
        return jnp.concatenate([tp[:, :, :-1], tp[:, :, 1:]], axis=3)

    kb = key_blocks(k)
    vb = key_blocks(v)
    i = jnp.arange(span)[:, None]
    c = jnp.arange(2 * span)[None, :]
    dist = i + span - c
    mk = jnp.arange(nb)[:, None, None] * span + c[None] - span
    valid = (dist >= 0)[None] & (dist <= span)[None] & (mk >= 0)
    bias = bias_g[t5_bucket(jnp.maximum(dist, 0) * dil)].transpose(2, 0, 1).astype(jnp.float32)
    logits = jnp.einsum('brnihd,brnjhd->brnhij', qb, kb, preferred_element_type=jnp.float32) + bias
    logits = jnp.where(valid[None, None, :, None], logits, -jnp.inf)
    m = jnp.max(logits, axis=-1, keepdims=True)
    p = jnp.exp(logits - m)
    s = jnp.sum(p, axis=-1)
    s_t = s.transpose(0, 1, 2, 4, 3)
    o = jnp.einsum('brnhij,brnjhd->brnihd', p, vb.astype(jnp.float32)) / s_t[..., None]
    lse = (m[..., 0] + jnp.log(s)).transpose(0, 1, 2, 4, 3)

    def back(t):
        t = t.reshape((B, dil, nb * span) + t.shape[4:])[:, :, :L]
        return jnp.moveaxis(t, 1, 2).reshape((B, S) + t.shape[3:])

    return back(o), back(lse)

def dilated_sample(q, k, v, buf, bias_g, window, dil):
    Bd, T, H, Dh = q.shape
    Wb = buf.shape[1]
    span = window // dil
    k_all = jnp.concatenate([buf[:, :, 0].astype(k.dtype), k], axis=1)
    v_all = jnp.concatenate([buf[:, :, 1].astype(v.dtype), v], axis=1)
    j = jnp.arange(span + 1)
    idx = jnp.arange(T)[:, None] + Wb - dil * j[None, :]
    valid = idx >= 0
    idx = jnp.maximum(idx, 0)
    kg = k_all[:, idx]
    vg = v_all[:, idx]
    bias = bias_g[t5_bucket(dil * j)].T.astype(jnp.float32)
    logits = jnp.einsum('bthd,btjhd->bthj', q, kg, preferred_element_type=jnp.float32) + bias
    logits = jnp.where(valid[None, :, None, :], logits, -jnp.inf)
    m = jnp.max(logits, axis=-1, keepdims=True)
    p = jnp.exp(logits - m)
    s = jnp.sum(p, axis=-1)
    o = jnp.einsum('bthj,btjhd->bthd', p, vg.astype(jnp.float32)) / s[..., None]
    lse = m[..., 0] + jnp.log(s)
    new_buf = jnp.stack([k_all[:, k_all.shape[1] - Wb:], v_all[:, v_all.shape[1] - Wb:]], axis=2)
    return o, lse, new_buf

def to_chunks(t, C):
    B, T = t.shape[0], t.shape[1]
    t = t.astype(jnp.float32).reshape((B, T // C, C) + t.shape[2:])
    return jnp.moveaxis(t, 3, 2).swapaxes(0, 1)

def from_chunks(t):
    t = jnp.moveaxis(t.swapaxes(0, 1), 2, 3)
    return t.reshape((t.shape[0], t.shape[1] * t.shape[2]) + t.shape[3:])

def gla_chunked(q, k, v, log_a, s0):
    T = q.shape[1]
    C = math.gcd(T, B_CHUNK)
    causal = jnp.tril(jnp.ones((C, C), dtype=bool))

    def step(S, inp):
        qc, kc, vc, ac = inp
        b = jnp.cumsum(ac, axis=2)
        diff = b[:, :, :, None, :] - b[:, :, None, :, :]
        dec = jnp.exp(jnp.where(causal[:, :, None], diff, -jnp.inf))
        att = jnp.einsum('bhtd,bhsd,bhtsd->bhts', qc, kc, dec)
        o = jnp.einsum('bhtd,bhdv->bhtv', qc * jnp.exp(b), S) + jnp.einsum('bhts,bhsv->bhtv', att, vc)
        b_last = b[:, :, -1:, :]
        S = jnp.exp(b_last[:, :, 0, :, None]) * S + jnp.einsum('bhsd,bhsv->bhdv', kc * jnp.exp(b_last - b), vc)
        return S, o

    S, o = lax.scan(step, s0.astype(jnp.float32),
                    (to_chunks(q, C), to_chunks(k, C), to_chunks(v, C), to_chunks(log_a, C)))
    return from_chunks(o), S

def gdn_chunked(q, k, v, g, beta, s0):
    T = q.shape[1]
    C = math.gcd(T, C_CHUNK)
    incl = jnp.tril(jnp.ones((C, C), dtype=bool))
    strict = jnp.tril(jnp.ones((C, C), dtype=bool), -1)
    eye = jnp.eye(C, dtype=jnp.float32)

    def step(S, inp):
        qc, kc, vc, gc, bc = inp
        b = jnp.cumsum(gc, axis=-1)
        dec = jnp.exp(jnp.where(incl, b[..., :, None] - b[..., None, :], -jnp.inf))
        kk = jnp.einsum('bhtd,bhsd->bhts', kc, kc)
        mat = eye + jnp.where(strict, bc[..., :, None] * dec * kk, 0.0)
        rhs = bc[..., None] * (vc - jnp.exp(b)[..., None] * jnp.einsum('bhtd,bhdv->bhtv', kc, S))
        u = lax.linalg.triangular_solve(mat, rhs, left_side=True, lower=True, unit_diagonal=True)
        qk = jnp.einsum('bhtd,bhsd->bhts', qc, kc)
        o = jnp.exp(b)[..., None] * jnp.einsum('bhtd,bhdv->bhtv', qc, S) + jnp.einsum('bhts,bhsv->bhtv', dec * qk, u)
        b_last = b[..., -1:]
        S = jnp.exp(b_last)[..., None] * S + jnp.einsum('bhsd,bhsv->bhdv', kc * jnp.exp(b_last - b)[..., None], u)
        return S, o

    S, o = lax.scan(step, s0.astype(jnp.float32),
                    (to_chunks(q, C), to_chunks(k, C), to_chunks(v, C), to_chunks(g, C), to_chunks(beta, C)))
    return from_chunks(o), S

def token_mixer(x, l, P, cache):
    B, T, _ = x.shape
    h = rms_norm(x, P['norm_mix'][l])
    z = jnp.einsum('btd,dn->btn', h, P['w_in'][l])
    a_q, a_k, a_v, b_q, b_k, b_v, b_g, b_lr, c_qkv, c_z, c_b, c_a, gates = jnp.split(z, split_points(), axis=-1)

    shp = (B, T, N_GROUPS, A_HEADS, A_DH)
    q = rms_norm(a_q.reshape(shp), P['a_q_norm'][l]) * (A_DH ** -0.5)
    k = rms_norm(a_k.reshape(shp), P['a_k_norm'][l])
    v = a_v.reshape(shp)
    outs, lses, bufs = [], [], []
    for g, (win, dil) in enumerate(A_GROUPS):
        bias_g = P['rel_bias'][:, g * A_HEADS:(g + 1) * A_HEADS]
        qg, kg, vg = q[:, :, g], k[:, :, g], v[:, :, g]
        if cache is None:
            o, lse = dilated_prompt(qg, kg, vg, bias_g, win, dil)
            wp = min(win, T)
            buf = jnp.stack([kg[:, T - wp:], vg[:, T - wp:]], axis=2)
        else:
            o, lse, buf = dilated_sample(qg, kg, vg, cache[0][g], bias_g, win, dil)
        outs.append(o)
        lses.append(lse)
        bufs.append(buf)
    wts = jax.nn.softmax(jnp.stack(lses, axis=0), axis=0)
    o_a = jnp.sum(wts[..., None] * jnp.stack(outs, axis=0), axis=0).reshape(B, T, A_WIDTH).astype(x.dtype)

    log_a = jax.nn.log_sigmoid((jnp.einsum('btr,rk->btk', b_lr, P['b_w_lr'][l]) + P['b_lr_bias'][l]).astype(jnp.float32)) / B_TAU
    s_b0 = jnp.zeros((B, B_HEADS, B_DK, B_DV), jnp.float32) if cache is None else cache[1]
    o_b, s_b = gla_chunked(b_q.reshape(B, T, B_HEADS, B_DK) * (B_DK ** -0.5), b_k.reshape(B, T, B_HEADS, B_DK),
                           b_v.reshape(B, T, B_HEADS, B_DV), log_a.reshape(B, T, B_HEADS, B_DK), s_b0)
    o_b = (rms_norm(o_b, P['b_out_norm'][l]) * jax.nn.silu(b_g.reshape(B, T, B_HEADS, B_DV).astype(jnp.float32)))
    o_b = o_b.reshape(B, T, BRANCH_W).astype(x.dtype)

    conv_buf = jnp.zeros((B, CONV_W - 1, C_CONV_CH), x.dtype) if cache is None else cache[3].astype(x.dtype)
    cat = jnp.concatenate([conv_buf, c_qkv], axis=1)
    w_conv = P['c_conv'][l]
    conv = jax.nn.silu(sum(cat[:, j:j + T] * w_conv[j] for j in range(CONV_W)))
    new_conv = cat[:, T:]
    cq, ck, cv = jnp.split(conv, [C_HEADS * C_DK, 2 * C_HEADS * C_DK], axis=-1)
    cq = l2_norm(cq.reshape(B, T, C_HEADS, C_DK)) * (C_DK ** -0.5)
    ck = l2_norm(ck.reshape(B, T, C_HEADS, C_DK))
    cv = cv.reshape(B, T, C_HEADS, C_DV)
    gdec = -jnp.exp(P['c_a_log'][l]) * jax.nn.softplus(c_a.astype(jnp.float32) + P['c_dt_bias'][l])
    beta = jax.nn.sigmoid(c_b.astype(jnp.float32))
    s_c0 = jnp.zeros((B, C_HEADS, C_DK, C_DV), jnp.float32) if cache is None else cache[2]
    o_c, s_c = gdn_chunked(cq, ck, cv, gdec, beta, s_c0)
    o_c = rms_norm(o_c, P['c_out_norm'][l]) * jax.nn.silu(c_z.reshape(B, T, C_HEADS, C_DV).astype(jnp.float32))
    o_c = o_c.reshape(B, T, BRANCH_W).astype(x.dtype)

    g_a, g_b, g_c = jnp.split(jax.nn.sigmoid(gates), 3, axis=-1)
    wb = P['w_branch'][l]
    merged = (g_a * jnp.einsum('btc,cd->btd', o_a, wb[0]) + g_b * jnp.einsum('btc,cd->btd', o_b, wb[1])
              + g_c * jnp.einsum('btc,cd->btd', o_c, wb[2]))
    out = jnp.einsum('btd,de->bte', merged, P['w_out'][l])
    return out, (tuple(bufs), s_b, s_c, new_conv)

def channel_mixer(x, l, P):
    h = rms_norm(x, P['norm_ffn'][l])
    i = l // 2
    if l % 2 == 0:
        a = jax.nn.silu(jnp.einsum('btd,df->btf', h, P['ffn_w_gate'][i])) * jnp.einsum('btd,df->btf', h, P['ffn_w_up'][i])
        return jnp.einsum('btf,fd->btd', a, P['ffn_w_down'][i])
    logits = jnp.einsum('btd,de->bte', h, P['moe_router'][i], preferred_element_type=jnp.float32)
    probs = jax.nn.softmax(logits, axis=-1)
    top_p, top_i = lax.top_k(probs, TOP_K)
    top_p = top_p / jnp.sum(top_p, axis=-1, keepdims=True)
    gate = jnp.sum(jax.nn.one_hot(top_i, N_EXPERTS, dtype=jnp.float32) * top_p[..., None], axis=-2)
    hg = jnp.einsum('btd,edf->btef', h, P['moe_w_gate'][i])
    hu = jnp.einsum('btd,edf->btef', h, P['moe_w_up'][i])
    a = jax.nn.silu(hg) * hu * gate[..., None].astype(h.dtype)
    return jnp.einsum('btef,efd->btd', a, P['moe_w_down'][i])

def setup_inputs(seed: int = 0) -> dict:
    key = jax.random.key(seed)
    ks = jax.random.split(key, 32)
    D = D_MODEL

    def nrm(k, shape, scale):
        return scale * jax.random.normal(k, shape, jnp.float32)

    def gain(k, shape):
        return 1.0 + 0.05 * jax.random.normal(k, shape, jnp.float32)

    def win_shape(w):
        return (DEPTH, DEC_BATCH, min(w, PAST_LEN), 2, A_HEADS, A_DH)

    dt = jnp.exp(jax.random.uniform(ks[18], (DEPTH, C_HEADS), jnp.float32, math.log(1e-3), math.log(1e-1)))
    return {
        'x_prompt': nrm(ks[0], (BATCH, SEQ, D), 1.0),
        'x_sample': nrm(ks[1], (DEC_BATCH, DEC_SEQ, D), 1.0),
        'cache_win128_kv': nrm(ks[2], win_shape(128), 1.0),
        'cache_win512_kv': nrm(ks[3], win_shape(512), 1.0),
        'cache_win2048_kv': nrm(ks[4], win_shape(2048), 1.0),
        'state_gla': nrm(ks[5], (DEPTH, DEC_BATCH, B_HEADS, B_DK, B_DV), 0.1),
        'state_gdn': nrm(ks[6], (DEPTH, DEC_BATCH, C_HEADS, C_DK, C_DV), 0.1),
        'state_conv': nrm(ks[7], (DEPTH, DEC_BATCH, CONV_W - 1, C_CONV_CH), 1.0),
        'norm_mix': gain(ks[8], (DEPTH, D)),
        'w_in': nrm(ks[9], (DEPTH, D, N_IN), D ** -0.5),
        'a_q_norm': gain(ks[10], (DEPTH, A_DH)),
        'a_k_norm': gain(ks[11], (DEPTH, A_DH)),
        'rel_bias': nrm(ks[12], (N_BUCKETS, N_GROUPS * A_HEADS), 0.5),
        'b_w_lr': nrm(ks[13], (DEPTH, B_RANK, B_HEADS * B_DK), B_RANK ** -0.5),
        'b_lr_bias': nrm(ks[14], (DEPTH, B_HEADS * B_DK), 0.1),
        'b_out_norm': gain(ks[15], (DEPTH, B_DV)),
        'c_conv': nrm(ks[16], (DEPTH, CONV_W, C_CONV_CH), CONV_W ** -0.5),
        'c_a_log': jnp.log(jax.random.uniform(ks[17], (DEPTH, C_HEADS), jnp.float32, 1.0, 16.0)),
        'c_dt_bias': dt + jnp.log(-jnp.expm1(-dt)),
        'c_out_norm': gain(ks[19], (DEPTH, C_DV)),
        'w_branch': nrm(ks[20], (DEPTH, 3, BRANCH_W, D), BRANCH_W ** -0.5),
        'w_out': nrm(ks[21], (DEPTH, D, D), D ** -0.5),
        'norm_ffn': gain(ks[22], (DEPTH, D)),
        'ffn_w_gate': nrm(ks[23], (N_DENSE, D, D_FF), D ** -0.5),
        'ffn_w_up': nrm(ks[24], (N_DENSE, D, D_FF), D ** -0.5),
        'ffn_w_down': nrm(ks[25], (N_DENSE, D_FF, D), D_FF ** -0.5),
        'moe_router': nrm(ks[26], (N_MOE, D, N_EXPERTS), D ** -0.5),
        'moe_w_gate': nrm(ks[27], (N_MOE, N_EXPERTS, D, D_FF_EXPERT), D ** -0.5),
        'moe_w_up': nrm(ks[28], (N_MOE, N_EXPERTS, D, D_FF_EXPERT), D ** -0.5),
        'moe_w_down': nrm(ks[29], (N_MOE, N_EXPERTS, D_FF_EXPERT, D), D_FF_EXPERT ** -0.5),
    }

def reference(x_prompt, x_sample, cache_win128_kv, cache_win512_kv, cache_win2048_kv, state_gla, state_gdn,
              state_conv, norm_mix, w_in, a_q_norm, a_k_norm, rel_bias, b_w_lr, b_lr_bias, b_out_norm, c_conv,
              c_a_log, c_dt_bias, c_out_norm, w_branch, w_out, norm_ffn, ffn_w_gate, ffn_w_up, ffn_w_down,
              moe_router, moe_w_gate, moe_w_up, moe_w_down):
    P = dict(norm_mix=norm_mix, w_in=w_in, a_q_norm=a_q_norm, a_k_norm=a_k_norm, rel_bias=rel_bias,
             b_w_lr=b_w_lr, b_lr_bias=b_lr_bias, b_out_norm=b_out_norm, c_conv=c_conv, c_a_log=c_a_log,
             c_dt_bias=c_dt_bias, c_out_norm=c_out_norm, w_branch=w_branch, w_out=w_out, norm_ffn=norm_ffn,
             ffn_w_gate=ffn_w_gate, ffn_w_up=ffn_w_up, ffn_w_down=ffn_w_down, moe_router=moe_router,
             moe_w_gate=moe_w_gate, moe_w_up=moe_w_up, moe_w_down=moe_w_down)
    xp, xs = x_prompt, x_sample
    new_p, new_s = [], []
    for l in range(DEPTH):
        out_p, st_p = token_mixer(xp, l, P, None)
        xp = xp + out_p
        xp = xp + channel_mixer(xp, l, P)
        new_p.append(st_p)
        cache_l = ((cache_win128_kv[l], cache_win512_kv[l], cache_win2048_kv[l]), state_gla[l], state_gdn[l], state_conv[l])
        out_s, st_s = token_mixer(xs, l, P, cache_l)
        xs = xs + out_s
        xs = xs + channel_mixer(xs, l, P)
        new_s.append(st_s)
    win128_p = jnp.stack([st[0][0] for st in new_p])
    win128_s = jnp.stack([st[0][0] for st in new_s])
    win512_p = jnp.stack([st[0][1] for st in new_p])
    win512_s = jnp.stack([st[0][1] for st in new_s])
    win2048_p = jnp.stack([st[0][2] for st in new_p])
    win2048_s = jnp.stack([st[0][2] for st in new_s])
    gla_p = jnp.stack([st[1] for st in new_p])
    gla_s = jnp.stack([st[1] for st in new_s])
    gdn_p = jnp.stack([st[2] for st in new_p])
    gdn_s = jnp.stack([st[2] for st in new_s])
    conv_p = jnp.stack([st[3] for st in new_p])
    conv_s = jnp.stack([st[3] for st in new_s])
    return (xp, xs, win128_p, win128_s, win512_p, win512_s, win2048_p, win2048_s,
            gla_p, gla_s, gdn_p, gdn_s, conv_p, conv_s)


_drawn_inputs = setup_inputs


def setup_inputs(seed=0):
    import zlib

    import numpy as np

    out = dict(_drawn_inputs(seed))
    spreads = {}
    factors = {}
    for name, (base, spread) in spreads.items():
        noise = np.random.default_rng([zlib.crc32(name.encode()), seed]).standard_normal(out[name].shape)
        drawn = base * np.exp(spread * noise) if base else spread * noise
        out[name] = __import__('jax').numpy.asarray(drawn.astype(out[name].dtype))
    for name, factor in factors.items():
        out[name] = (out[name] * factor).astype(out[name].dtype)
    return out
```

```python
from contextlib import ExitStack

import concourse.bass as bass
from concourse import mybir

F32 = mybir.dt.float32
ALU = mybir.AluOpType
ACT = mybir.ActivationFunctionType
AX = mybir.AxisListType

P = 128
D = 1024
KT = D // P
NP_TOK = 256
NS = 8
T = NP_TOK + NS
TT = NP_TOK // P
DEPTH = 2
GROUPS = ((128, 1), (512, 4), (2048, 16))
NG = 3
AH, DH = 8, 64
BH, BDK, BDV, BRANK, BTAU, BC = 4, 64, 128, 16, 16.0, 64
CH, CD, CONVW, CCH = 4, 128, 4, 1536
FF, FE, NE = 2816, 1792, 8
NB = 32
EPS = 1e-6
NEG = -1e30

Z_C, Z_CZ, Z_BQ, Z_BK, Z_BV, Z_BG, Z_Q, Z_K, Z_V, Z_G, Z_N = 0, 12, 16, 18, 20, 24, 28, 40, 52, 64, 88
W_RUNS = ((Z_C, 6160), (Z_BQ, 4608), (Z_Q, 0), (Z_G, 8216))

CW = 2048
RING = 5
RING_F = 7

R_NM, R_NF, R_LRB, R_BO, R_CO, R_CV, R_QN, R_KN, R_N = 0, 8, 16, 18, 19, 20, 68, 69, 70

K_NAMES = ["ident", "ones", "blk", "upper", "neg_t", "pos_s", "m16", "m16t", "m32t", "m64t", "m128t", "hmap",
           "gla", "iota", "hsel", "bsel", "esel"]
K_W = dict(hmap=512, hsel=24, bsel=8, esel=64)
K_OFF = {}
_o = 0
for _n in K_NAMES:
    K_OFF[_n] = _o
    _o += K_W.get(_n, 128)
K_TOT = _o
S_TAB, S_KEY, S_SELF, S_TOT = 0, NG * 512, NG * 512 + NG * P, NG * 512 + NG * P + NS

CH_PROJ, CH_WB, CH_WO = Z_N // 2, 6, 4
CH_MIX = CH_PROJ + CH_WB + CH_WO
CH_FFG, CH_FFD = 22, 11
CH_EG, CH_ED = 14, 7
N_EXP_CH = CH_EG + CH_ED


def w_in_col(tile):
    start, col = [r for r in W_RUNS if r[0] <= tile][-1]
    return col + (tile - start) * P


def schedule(l):
    s = [("xnorm", 0), ("small",)]
    proj = iter(range(Z_N))

    def stream(n):
        return [("proj", next(proj)) for _ in range(n)]

    s += stream(16)
    s += [("conv",)]
    s += stream(2)
    s += [("gate_c",)]
    s += stream(2)
    s += [("norm4", 0), ("norm4", 1)]
    for i in range(TT):
        s += [("gdn_dec", i)] + stream(1) + [("gdn_a", i)] + stream(1)
        for q in range(3):
            s += [("gdn_sq", i, q)] + stream(1)
        for v in range(3):
            s += [("gdn_lv", i, v)] + stream(1)
        s += [("gdn_st", i)] + stream(1)
    s += [("gdn_s",), ("bar", 0), ("norm4", 2), ("bar", 1)]
    s += stream(1)
    s += [("gla_la",), ("gla_prep",)]
    for i in range(TT):
        s += [("gla_at", i)] + stream(1)
    for c in range(4):
        s += [("gla_ch", c)] + stream(2)
    s += [("gla_s",), ("norm4", 3), ("bar", 2)]
    s += stream(64 - 20 - 2 * 9 - 1 - 2 - 8)
    s += [("norm4", 4 + n) for n in range(6)]
    s += [("kv_tok",)]
    for h in range(AH):
        s += [("att", h)] + stream(3)
    s += [("bar", 3), ("att_s",)]
    s += list(stream(0))
    s += [("sig",), ("bar", 4), ("merge",)]
    assert next(proj, None) is None
    return s


def mixer_jobs(step):
    k, a = step[0], step[1:]
    if k == "xnorm":
        return [("xn", *a)]
    if k == "small":
        return [("par",), ("ab",), ("cba",), ("lr",)]
    if k == "proj":
        return [("p", *a)]
    if k == "conv":
        return [("cs",), ("co", 0), ("co", 1), ("co", 2)]
    if k == "gate_c":
        return [("btok",)]
    if k == "norm4":
        return [("n4", a[0], t) for t in range(4)]
    if k == "gdn_dec":
        return [("brow", *a)]
    if k == "gdn_a":
        return [("kk", *a), ("qk", *a), ("at", *a)]
    if k == "gdn_sq":
        return [("sq0", *a)] + [("sq1", *a)] * (a[1] < 2) + [("xx0", *a), ("xx1", *a)]
    if k == "gdn_lv":
        return [("y", *a)] + [("lx0", *a)] * (a[1] < 2) + [("lx1", *a)]
    if k == "gdn_st":
        return [("vt", *a)] + [("ks", *a)] * (a[0] > 0) + [("u", *a), ("oc", *a), ("kt", *a), ("ds", *a)]
    if k == "gdn_s":
        return [("skq",), ("sqk",), ("sgb",), ("suk",)] + [("su", n) for n in range(8)]
    if k == "gla_la":
        return [("la", 0), ("la", 1)]
    if k == "gla_prep":
        return [("vb", 0), ("vb", 1), ("ket",)]
    if k == "gla_at":
        return [("ga", *a), ("go", *a)]
    if k == "gla_ch":
        return [("gi", *a)] * (a[0] > 0) + [("gs", *a)]
    if k == "gla_s":
        return [("gk",), ("gv",)] + [("gu", n) for n in range(4)] + [("gq", w) for w in range(2)]
    if k == "kv_tok":
        return [("tk", i, n) for i in range(TT) for n in range(6)]
    if k == "att":
        return [(n, a[0], i, *x) for i in range(TT) for n, x in
                ([("sc", (0,))] + [("sc", (1,))] * i + [("pt", (q,)) for q in range(1 + i)] + [("pv", ())])] + (
                    [("oa", i) for i in range(TT)] if a[0] == AH - 1 else [])
    if k == "att_s":
        return ([("ts", n) for n in range(9)] + [("qb", n) for n in range(NG * NS)]
                + [("sx",), ("lt",), ("pk",), ("rr",), ("pvs",)])
    if k == "merge":
        return [("mb", b, d) for b in range(3) for d in range(KT)] + [("wo", d) for d in range(KT)]
    return []


PER = dict(
    h_ready=2, sq_ready=2, rs_ready=2, sq4=10, rs4=10, n4_done=10, par_ready=1, lr_ready=1,
    xa_ready=1, g_exp=1, g_ready=1, conv_sum=1, conv_sig=1, conv_done=1, cz_sig=1, btok_ready=1, cst_ready=1,
    ebr_ready=2, t1_ready=2, dec_ready=2, x0_ready=2, ot_ready=6, r_ready=2, qe_ready=1, dlx_ready=2, dl_ready=2,
    gs_k=1, gs_prod=1, gs_eg=1, gs_d=1, gs_o=1, um_ready=4, s_state=1, s_new=1,
    la_x=1, la_e=1, b_ready=1, eb_ready=1, ke_ready=1, gla_state=4, bg_sig=1,
    vm_ready=4, g_new=1,
    sc_add=16, p_ready=16, rs_inv=16, kst_ready=6,
    l_ready=1, ls_ready=1, sp_max=1, ps_ready=1, dd_ready=1, v_used=8, oas_ready=1,
    sig_ready=1, acc_ready=1, bar_v=5, bar_a=5, bar_p=5, cz_done=1, s_o=1,
)


def constants():
    import math
    import numpy as np
    c = np.zeros((P, K_TOT), np.float32)

    def put(name, a):
        c[:a.shape[0], K_OFF[name]:K_OFF[name] + a.shape[1]] = a

    r = np.arange(P)
    row, col = r[:, None], r[None, :]
    put("ident", np.eye(P))
    put("ones", np.ones((P, P)))
    put("blk", (row // 64 == col // 64) * 1.0)
    put("upper", (row <= col) * 1.0)
    put("neg_t", np.where(row <= col, 0.0, NEG))
    put("pos_s", np.where(col < row, 0.0, -NEG))
    low = col < row
    put("m16", (low & (row // 16 == col // 16)) * 1.0)
    put("m16t", (low & (row // 16 == col // 16)).T * 1.0)
    for b in (32, 64, 128):
        m = low & (row // b == col // b) & (row // (b // 2) != col // (b // 2))
        put(f"m{b}t", m.T * 1.0)
    put("gla", ((row <= col) & (row // BC == col // BC)) * 1.0)
    put("iota", np.broadcast_to(r, (P, P)))
    bh = np.arange(64)[:, None]
    put("hmap", (bh % 8 == np.arange(512)[None] // 64) * 1.0)
    put("hsel", (bh % 8 == np.arange(24)[None] % 8) * 1.0)
    put("bsel", (bh // 8 == np.arange(8)[None]) * 1.0)
    put("esel", (np.arange(8)[:, None] == np.arange(64)[None] // 8) * 1.0)

    def bucket(dist):
        d = np.maximum(dist.astype(np.float32), np.float32(1.0))
        big = 16 + (np.log(d / np.float32(16)) / np.float32(math.log(128.0)) * 16).astype(np.int32)
        return np.where(dist < 16, dist, np.minimum(big, 31))

    s = np.zeros((NB + 1, S_TOT), np.float32)
    m = np.arange(512)
    dist = 128 - np.where(m < 256, m, m - 512)
    for g, (win, dil) in enumerate(GROUPS):
        ok = (dist >= 0) & (dist % dil == 0) & (dist <= win)
        b = bucket(np.maximum(dist, 0))
        s[np.where(ok, b, NB), S_TAB + 512 * g + m] = 1.0
        key = np.arange(P)
        s[bucket(win - key * dil), S_KEY + P * g + key] = 1.0
    s[NB, :S_KEY] *= NEG
    s[0, S_SELF:] = 1.0
    return c, s


def build(nc, a, o):
    ctx = ExitStack()
    with ctx:
        def sb(name, shape):
            return ctx.enter_context(nc.sbuf_tensor(name, shape, F32))

        def sem(name):
            return ctx.enter_context(nc.semaphore(name))

        ring = sb("ring", [P, RING, CW])
        z = sb("z", [P, Z_N, T])
        x = sb("x", [P, KT, T])
        h = sb("h", [P, KT, T])
        con = sb("con", [P, K_TOT])
        arena = sb("arena", [P, 11100])
        small = sb("small", [P, 1700])
        PS = ctx.enter_context(nc.psum_tensor("PS", [P, 8, 512], F32))

        def K(name, rows=P, w=None):
            return con[0:rows, K_OFF[name]:K_OFF[name] + (w or K_W.get(name, P))]

        ident, ones = K("ident"), K("ones")
        zs = z[:, 0:8, :].rearrange("p a b -> p (a b)")

        class Cut:
            def __init__(self, base, at=0):
                self.base, self.at = base, at

            def take(self, n, rows=P):
                v = self.base[0:rows, self.at:self.at + n]
                self.at += n
                assert self.at <= self.base.shape[1], (self.at, self.base.shape)
                return v

        def v3(ap, n):
            return ap.rearrange("p (a b) -> p a b", a=n)

        cs = Cut(small)
        par = cs.take(R_N)
        rs = cs.take(T)
        cba = v3(cs.take(24), 3)
        ab = cs.take(8)
        beta = v3(cs.take(12), 3)
        xa = v3(cs.take(12), 3)
        gabs = v3(cs.take(12), 3)
        gl = v3(cs.take(12), 3)
        ealog = cs.take(4)
        btok, nbtok, ebtok, nebtok = cs.take(8), cs.take(8), cs.take(8), cs.take(8)
        blast, eblast, dl = cs.take(4), cs.take(4), cs.take(4)
        rowmax, rowsum, rowinv = cs.take(16), cs.take(16), cs.take(16)
        prow = cs.take(P)
        arow = cs.take(8, 1)
        wsm = v3(cs.take(192), KT)
        wlr = cs.take(256, BRANK)
        lr = cs.take(T, BRANK)
        relb = cs.take(24, NB + 1)
        biask, bself = cs.take(24), cs.take(24, NS)
        qnw = cs.take(1)

        cc = Cut(arena)
        c = v3(cc.take(12 * T), 12)
        ebr, t1, A, QK, AT, Pm, PT, X, XT, qe, S = [v3(cc.take(512), 4) for _ in range(11)]
        ucat = cc.take(12 * 32)
        catS = ucat.rearrange("p (j b k) -> p j b k", j=12, b=8)
        convt = cc.take(CCH, 24)
        s_bc = cc.take(64).rearrange("p (n b h) -> p n b h", n=2, b=8)
        s_u = cc.take(32)
        s_k = cc.take(32)
        s_t = cc.take(32)
        s_q = cc.take(32)
        s_d = cc.take(64, 8)
        s_eg = cc.take(4)
        zc = Cut(zs)
        Y, R, U, kd = [v3(zc.take(512), 4) for _ in range(4)]
        S0 = arena[:, 12 * T + 1024:12 * T + 1024 + 4096].rearrange("p (n v) -> p n v", v=CD)
        um = [zs[0:32, 1024 * n:1024 * n + 1024].rearrange("p (a v) -> p a v", v=CD) for n in range(2)]
        uk_sb = arena[0:32, 12 * T + 1024 - 512:12 * T + 1024 - 256]

        cb = Cut(arena)
        la = v3(cb.take(2 * T), 2)
        lax = v3(cb.take(2 * T), 2)
        laa = v3(cb.take(2 * T), 2)
        gb, geb, keg = [v3(cb.take(512), 2) for _ in range(3)]
        qz = v3(cb.take(1024), BH)
        vb = v3(cb.take(1024), 2)
        ket = v3(cb.take(512), 2)
        gatt = v3(cb.take(512), BH)
        GS = v3(cb.take(256), 2)
        ob = v3(cb.take(4 * T), 4)
        g_s0 = cb.take(2048).rearrange("p (q b v) -> p q b v", q=2, b=8)
        g_k, g_v = cb.take(256, 8), cb.take(512, 8)
        vm = [zs[0:8, 1024 * n:1024 * n + 1024].rearrange("p (b v) -> p b v", b=8) for n in range(2)]
        g_a = cb.take(16)

        ca = Cut(arena)
        vtok = v3(ca.take(TT * 1536), TT)
        sc = [ca.take(768) for _ in range(2)]
        pt = [ca.take(768) for _ in range(2)]
        btab = [v3(ca.take(768), NG) for _ in range(2)]
        kst = [ca.take(512) for _ in range(2)]
        oat = v3(ca.take(1024), TT)
        oaT = z[:, Z_BV:Z_BV + 4, :]
        cz = Cut(arena)
        tok = cz.take(36 * P, 8)
        tok_g = tok.rearrange("p (w g x) -> p w g x", w=3, g=NG)
        cache = [cz.take(512) for _ in range(6)]
        prod = [cz.take(512) for _ in range(2)]
        L = cz.take(192)
        sp_ = cz.take(NG * P + NG, 64)
        sself = cz.take(24, 8)
        sself2 = cz.take(24, 64)
        pts = cz.take(192)
        dd = v3(cz.take(32, 64), 4)
        rrs = cz.take(128)
        vprod = cz.take(32)

        sems = {n: sem(n) for n in PER}
        bank_full = [sem(f"bank_full{b}") for b in range(8)]
        bank_free = [sem(f"bank_free{b}") for b in range(8)]
        landed = [sem(f"landed{r}") for r in range(RING_F)]
        con_in, setup_in, relb_in, prow_in, wsm_in, wlr_in, convt_in = [
            sem(n) for n in ("con_in", "setup_in", "relb_in", "prow_in", "wsm_in", "wlr_in", "convt_in")]
        x_in, x_first, x_done = sem("x_in"), sem("x_first"), sem("x_done")
        tab_row, tab_out, tab_in = sem("tab_row"), [sem("tab_out0"), sem("tab_out1")], [sem("tab_in0"), sem("tab_in1")]
        s0_in, gs0_in = sem("s0_in"), sem("gs0_in")
        cache_in = [sem(f"cache_in{n}") for n in range(6)]
        stored = {n: sem(f"stored_{n}") for n in ("k0", "k1", "v", "conv", "gdn", "gdns", "gla", "glas", "toks", "copy", "y")}
        vec, act_s = sem("vec_chain"), sem("act_chain")
        down_used = sem("down_used")
        silu_done, router_in, r_exp, r_gate = sem("silu_done"), sem("router_in"), sem("r_exp"), sem("r_gate")
        relb_one, silu_used, r_max = sem("relb_one"), sem("silu_used"), sem("r_max")
        r_mask, r_flag, r_slots, r_back = sem("r_mask"), sem("r_flag"), sem("r_slots"), sem("r_back")
        epsc = EPS

        def V(name, l, i=0):
            assert 0 <= i < PER[name]
            return l * PER[name] + i + 1

        JOB, used, turn = {}, [0] * 8, [0]

        def plan(job, bank=None):
            if bank is None:
                bank = 2 + turn[0] % 6
                turn[0] += 1
            assert job not in JOB
            JOB[job] = (bank, used[bank])
            used[bank] += 1

        SCHED = [schedule(l) for l in range(DEPTH)]
        TOKS = [(0, P), (P, P), (NP_TOK, NS)]
        for n in range(8):
            plan(("x0", n), n)
        for n in range(24):
            plan(("tab", n), n % 8)
        plan(("bs",), 0)
        plan(("bself",), 1)
        for l in range(DEPTH):
            for step in SCHED[l]:
                for job in mixer_jobs(step):
                    plan((l, *job), job[1] % 2 if job[0] == "p" else None)
            plan((l, "xn", 1))
            if l == 0:
                for i in range(FF // P):
                    plan((0, "fg", i), 2 * (i % 2))
                    plan((0, "fu", i), 2 * (i % 2) + 1)
                for d in range(KT):
                    plan((0, "fd", d), d)
            else:
                plan((1, "rl", 0), 0)
                plan((1, "rt", 0), 1)
                plan((1, "gt", 0), 2)
                plan((1, "rp", 0), 3)
                for n in range(2 * len(TOKS)):
                    plan((1, "ht", n), 4 + n % 4)
                for n in range(NE):
                    plan((1, "st", n), n)
                moe_base = list(used)
                for i in range(FE // P):
                    plan((1, "fg", i), 2 * (i % 2))
                    plan((1, "fu", i), 2 * (i % 2) + 1)
                plan((1, "gh", 0), 4)
                plan((1, "gh", 1), 5)
                plan((1, "dn", 0), 6)
                plan((1, "dn", 1), 7)
                for d in range(KT):
                    plan((1, "fd", d), d)
                moe_per = [used[b] - moe_base[b] for b in range(8)]
                used = [moe_base[b] + NE * moe_per[b] for b in range(8)]
        for i in range(2 * (TT + 1)):
            plan(("y", i), i)

        def bank(*job):
            return PS[:, JOB[job][0], :]

        def open_bank(pe, *job, e=None):
            b, m = JOB[job]
            if e is not None:
                pe.wait_ge(bank_free[b], e * moe_per[b] + m)
            elif m:
                pe.wait_ge(bank_free[b], m)

        def full(*job):
            return bank_full[JOB[job][0]]

        def free(*job):
            return bank_free[JOB[job][0]]

        def wait_full(eng, *job, e=None):
            b, m = JOB[job]
            eng.wait_ge(bank_full[b], m + 1 if e is None else e * moe_per[b] + (m + 1))

        def wait_read(eng, *job, e=None):
            b, m = JOB[job]
            eng.wait_ge(bank_free[b], m + 1 if e is None else e * moe_per[b] + (m + 1))

        def wait_z(eng, l, lo, hi):
            for j in range(max(lo, hi - 2), hi):
                wait_read(eng, l, "p", j)

        CH0 = [0, CH_MIX + CH_FFG + CH_FFD]
        MOE0 = CH0[1] + CH_MIX
        CHUNK, loads, held = {}, [0] * RING_F, [None] * RING_F

        def place(n, s_, last):
            CHUNK[n] = (s_, loads[s_], held[s_])
            loads[s_] += 1
            held[s_] = last

        for l in range(DEPTH):
            n0 = CH0[l]
            for q in range(CH_PROJ):
                place(n0 + q, q % RING, (l, "p", 2 * q + 1))
            for q in range(CH_WB):
                place(n0 + CH_PROJ + q, (CH_PROJ + q) % RING, (l, "mb", q // 2, KT - 1))
            for q in range(CH_WO):
                n = CH_PROJ + CH_WB + q
                place(n0 + n, n % RING, (l, "wo", 2 * q + 1))
            if l == 0:
                for q in range(CH_FFG):
                    place(CH_MIX + q, q % RING_F, (0, "fu" if q % 2 else "fg", 2 * (q // 2) + 1))
                for q in range(CH_FFD):
                    place(CH_MIX + CH_FFG + q, (CH_FFG + q) % RING_F,
                          ("down", q + 1) if q < CH_FFD - 1 else (0, "fd", KT - 1))
        DOWN0 = CH_FFD - 1
        moe_loads = list(loads)
        for q in range(RING_F):
            CHUNK[MOE0 + q] = (q, loads[q], held[q])

        def moe_last(q):
            if q < CH_EG:
                return (1, "fu" if q % 2 else "fg", 2 * (q // 2) + 1)
            return ("down", q - CH_EG + 1) if q < N_EXP_CH - 1 else (1, "fd", KT - 1)

        def slot_ap(s_):
            return ring[:, s_, :] if s_ < RING else arena[:, (s_ - RING) * CW:(s_ - RING + 1) * CW]

        def chunk(n):
            return slot_ap(CHUNK[n][0])

        def wait_chunk(pe, n):
            s_, m, _ = CHUNK[n]
            pe.wait_ge(landed[s_], 16 * (m + 1))

        dscr = nc.dram_tensor("bias_tables", [24, P, 512], F32, kind="Internal").ap()

        fa = z[:, 8:8 + FF // P, :]
        fs = z[:, 32:36, :]
        ft = z[:, 36:40, :]
        gB = z[:, 48:50, :]
        wr = z[:, 50, 0:64]
        rlog = z[:, 51, :]
        gT = z[:, 54, :]
        rt = Cut(z[:, 52:54, :].rearrange("p a b -> p (a b)"))
        rl, rl2, req, rcum, rf1, rf2, rg = [v3(rt.take(24), 3) for _ in range(7)]
        rm1, rm2, rexp, rden = [rt.take(3) for _ in range(4)]
        rmask, rpos = [v3(rt.take(24), 3) for _ in range(2)]
        rmost = rt.take(1)
        gw = [v3(z[:, 40 + 2 * n:42 + 2 * n, :].rearrange("p a b -> p (a b)")[:, 0:3 * P], 3) for n in range(2)]
        htok = v3(arena[:, 2 * CW:2 * CW + 3 * D], 3)
        G = arena[:, 2 * CW + 3 * D:2 * CW + 6 * D].rearrange("p (i e s) -> p i e s", i=3, e=NE)
        ST = z[:, 72:80, :]
        hs = v3(z[:, 80:84, :].rearrange("p a b -> p (a b)")[:, 0:D], KT)
        ys = z[:, 84:88, :].rearrange("p a b -> p (a b)")[:, 0:D]
        crowded = ctx.enter_context(nc.sbuf_tensor("crowded", [1, 1], mybir.dt.int32))
        yst = [z[:, 56 + 4 * n:60 + 4 * n, :].rearrange("p a b -> p (a b)")[:, 0:D] for n in range(3)]

        xst = [arena[:, D * n:D * n + D] for n in range(3)]
        setup = arena[0:NB + 1, 3 * D:3 * D + S_TOT]
        ztab = z[:, 40:, :].rearrange("p a b -> p (a b)")[:, 0:24 * 512].rearrange("p (n c) -> p n c", n=24)
        g8 = z[0:NE, 64:72, :]

        def bc(ap, axis, shape):
            return ap.unsqueeze(axis).to_broadcast(shape)

        N4 = ([(c, 4 * n, "ones", 1.0, None) for n in range(2)] + [(c, 8, "ones", 1.0 / CD, par[:, R_CO:R_CO + 1])]
              + [(ob, 0, "ones", 1.0 / BDV, par[:, R_BO:R_BO + 1])]
              + [(z, Z_Q + 4 * n, "blk", 1.0 / DH, qnw if n < 3 else par[:, R_KN:R_KN + 1]) for n in range(6)])
        LAST_SRC = None

        def sq4(n):
            return z[:, 4 * (n % 2):4 * (n % 2) + 4, :]

        block = ctx.enter_context(nc.Block())

        @block.sync
        def _(sp):
            def source(l, n):
                if n < CH_PROJ:
                    col = w_in_col(2 * n)
                    return a["w_in"][l].rearrange("(k p) n -> p k n", p=P)[:, :, col:col + 256]
                n -= CH_PROJ
                if n < CH_WB:
                    return a["w_branch"][l, n // 2].rearrange("(k p) n -> p k n", p=P)[:, 2 * (n % 2):2 * (n % 2) + 2, :]
                n -= CH_WB
                if n < CH_WO:
                    return a["w_out"][l].rearrange("(k p) n -> p k n", p=P)[:, :, 256 * n:256 * n + 256]
                n -= CH_WO
                if n < CH_FFG:
                    w = a["ffn_w_up" if n % 2 else "ffn_w_gate"][0]
                    return w.rearrange("(k p) n -> p k n", p=P)[:, :, 256 * (n // 2):256 * (n // 2) + 256]
                n -= CH_FFG
                return a["ffn_w_down"][0].rearrange("(k p) n -> p k n", p=P)[:, 2 * n:2 * n + 2, :]

            def load(n, src):
                s_, m, before = CHUNK[n]
                if before is not None and before[0] == "down":
                    sp.wait_ge(down_used, before[1])
                elif before is not None:
                    wait_full(sp, *before)
                k = 2 if src.shape[1] == 2 else KT
                sp.dma_start(v3(slot_ap(s_), k), src).then_inc(landed[s_], 16)

            def expert(e, q):
                if q < CH_EG:
                    w = a["moe_w_up" if q % 2 else "moe_w_gate"][0]
                    return w[e].rearrange("(k p) n -> p k n", p=P)[:, :, 256 * (q // 2):256 * (q // 2) + 256]
                q -= CH_EG
                return a["moe_w_down"][0][e].rearrange("(k p) n -> p k n", p=P)[:, 2 * q:2 * q + 2, :]

            def load_e(e, q):
                before = moe_last((q - RING_F + (q == CH_EG - 1)) % N_EXP_CH)
                if q == CH_EG:
                    pass
                elif before[0] == "down":
                    sp.wait_ge(down_used, e * (CH_ED - 1) + (DOWN0 + before[1]))
                else:
                    wait_full(sp, *before, e=e)
                src = expert(e if q >= RING_F else e + 1, q)
                sp.dma_start(v3(slot_ap(q % RING_F), src.shape[1]), src).then_inc(landed[q % RING_F], 16)

            sp.dma_start(con[:, :], a["const_main"]).then_inc(con_in, 16)
            for l in range(DEPTH):
                for n in range(CH_MIX + (CH_FFG + CH_FFD if l == 0 else 0)):
                    if l == 0 and n == CH_MIX + RING:
                        sp.wait_ge(sems["bar_v"], V("bar_v", 0, 4))
                        sp.wait_ge(sems["bar_a"], V("bar_a", 0, 4))
                    load(CH0[l] + n, source(l, n))
            for q in range(RING_F):
                if q == RING:
                    sp.wait_ge(sems["bar_v"], V("bar_v", 1, 4))
                    sp.wait_ge(sems["bar_a"], V("bar_a", 1, 4))
                load(MOE0 + q, expert(0, q))
            with sp.Fori(0, NE - 1) as e:
                for q in range(RING_F, N_EXP_CH):
                    load_e(e, q)
                for q in range(RING_F):
                    load_e(e, q)
            for q in range(RING_F, N_EXP_CH):
                load_e(NE - 1, q)
            for name, n in STORES.items():
                sp.wait_ge(stored[name], 16 * n)

        @block.tensor
        def _(pe):
            mm, tr = nc.tensor.matmul, nc.tensor.transpose

            def turn_over(out, in_, rows, **kw):
                return tr(out, in_, ident[0:rows, 0:rows])

            def dense(job, w, l, e=None):
                for k in range(KT):
                    last = mm(bank(*job)[:, 0:T], w(k), h[:, k, :], start=(k == 0), stop=(k == KT - 1))
                last.then_inc(full(*job), 1)

            def xnorm(l, w):
                pe.wait_ge(sems["sq_ready"], V("sq_ready", l, w))
                open_bank(pe, l, "xn", w)
                for k in range(KT):
                    last = mm(bank(l, "xn", w)[:, 0:T], ones, z[:, k, :], start=(k == 0), stop=(k == KT - 1))
                last.then_inc(full(l, "xn", w), 1)

            def small_step(l):
                pe.wait_ge(prow_in, 192 * (l + 1))
                open_bank(pe, l, "par")
                turn_over(bank(l, "par")[:, 0:R_N], prow[0:R_N, :], R_N).then_inc(full(l, "par"), 1)
                open_bank(pe, l, "ab")
                mm(bank(l, "ab")[:, 0:8], ones[0:1, :], arow, start=True, stop=True).then_inc(full(l, "ab"), 1)
                pe.wait_ge(wsm_in, 32 * (l + 1))
                pe.wait_ge(sems["h_ready"], V("h_ready", l, 0))
                open_bank(pe, l, "cba")
                for i, (t0, nt) in enumerate(TOKS):
                    for k in range(KT):
                        last = mm(bank(l, "cba")[0:nt, 8 * i:8 * i + 8], h[:, k, t0:t0 + nt], wsm[:, k, 16:24],
                                  start=(k == 0), stop=(k == KT - 1))
                last.then_inc(full(l, "cba"), 1)
                open_bank(pe, l, "lr")
                for k in range(KT):
                    last = mm(bank(l, "lr")[0:BRANK, 0:T], wsm[:, k, 0:BRANK], h[:, k, :],
                              start=(k == 0), stop=(k == KT - 1))
                last.then_inc(full(l, "lr"), 1)

            def proj(l, j):
                n = CH0[l] + j // 2
                if j % 2 == 0:
                    wait_chunk(pe, n)
                open_bank(pe, l, "p", j)
                w = v3(chunk(n), KT)
                dense((l, "p", j), lambda k: w[:, k, (j % 2) * P:(j % 2 + 1) * P], l)

            def conv(l):
                pe.wait_ge(convt_in, 16 * (l + 1))
                open_bank(pe, l, "cs")
                for j in range(12):
                    last = turn_over(bank(l, "cs")[:, 24 * j:24 * j + 24], convt[:, P * j:P * j + P], 24)
                last.then_inc(full(l, "cs"), 1)
                wait_z(pe, l, 0, 12)
                for q in range(3):
                    open_bank(pe, l, "co", q)
                    for j in range(4):
                        last = turn_over(bank(l, "co", q)[0:11, P * j:P * j + P], z[:, 4 * q + j, 253:T], P)
                    last.then_inc(full(l, "co", q), 1)

            def gate_c(l):
                pe.wait_ge(sems["g_ready"], V("g_ready", l))
                open_bank(pe, l, "btok")
                mm(bank(l, "btok")[:, 0:8], K("upper"), gl[:, 0:2, :].rearrange("p a b -> p (a b)"),
                   start=True, stop=True).then_inc(full(l, "btok"), 1)

            def norm4(l, n):
                pe.wait_ge(sems["sq4"], V("sq4", l, n))
                for t in range(4):
                    open_bank(pe, l, "n4", n, t)
                    mm(bank(l, "n4", n, t)[:, 0:T], K(N4[n][2]), sq4(n)[:, t, :], start=True, stop=True).then_inc(
                        full(l, "n4", n, t), 1)

            def heads(job, left, right):
                open_bank(pe, *job)
                for q in range(CH):
                    last = mm(bank(*job)[:, P * q:P * q + P], left(q), right(q), start=True, stop=True)
                last.then_inc(full(*job), 1)

            def gdn_dec(l, i):
                heads((l, "brow", i), lambda q: gl[:, i, q:q + 1].to_broadcast([P, P]), lambda q: K("upper"))

            def gdn_a(l, i):
                tok_ = slice(P * i, P * i + P)
                pe.wait_ge(sems["n4_done"], V("n4_done", l, 1))
                heads((l, "kk", i), lambda q: c[:, 4 + q, tok_], lambda q: c[:, 4 + q, tok_])
                heads((l, "qk", i), lambda q: c[:, 4 + q, tok_], lambda q: c[:, q, tok_])
                wait_read(pe, l, "kk", i)
                job = (l, "at", i)
                open_bank(pe, *job)
                for q in range(CH):
                    last = turn_over(bank(*job)[:, P * q:P * q + P], A[:, q, :], P)
                last.then_inc(full(*job), 1)

            def gdn_sq(l, i, q):
                if q == 0:
                    pe.wait_ge(sems["x0_ready"], V("x0_ready", l, i))
                else:
                    wait_read(pe, l, "sq0", i, q - 1)
                    wait_read(pe, l, "sq1", i, q - 1)
                heads((l, "sq0", i, q), lambda n: PT[:, n, :], lambda n: Pm[:, n, :])
                if q < 2:
                    heads((l, "sq1", i, q), lambda n: Pm[:, n, :], lambda n: PT[:, n, :])
                wait_read(pe, l, "sq0", i, q)
                if q:
                    wait_read(pe, l, "xx1", i, q - 1)
                heads((l, "xx0", i, q), lambda n: XT[:, n, :], lambda n: Pm[:, n, :])
                heads((l, "xx1", i, q), lambda n: Pm[:, n, :], lambda n: XT[:, n, :])

            def gdn_lv(l, i, v):
                pe.wait_ge(sems["ot_ready"], V("ot_ready", l, 3 * i + v))
                wait_read(pe, l, *(("xx0", i, 2) if v == 0 else ("lx0", i, v - 1)))
                heads((l, "y", i, v), lambda n: t1[:, n, :], lambda n: X[:, n, :])
                wait_read(pe, l, "y", i, v)
                wait_read(pe, l, *(("xx1", i, 2) if v == 0 else ("lx1", i, v - 1)))
                if v < 2:
                    heads((l, "lx0", i, v), lambda n: XT[:, n, :], lambda n: Y[:, n, :])
                heads((l, "lx1", i, v), lambda n: Y[:, n, :], lambda n: XT[:, n, :])

            def gdn_st(l, i):
                tok_ = slice(P * i, P * i + P)

                def turned(name, base):
                    open_bank(pe, l, name, i)
                    for q in range(CH):
                        last = turn_over(bank(l, name, i)[:, P * q:P * q + P], c[:, base + q, tok_], P)
                    last.then_inc(full(l, name, i), 1)

                turned("vt", 8)
                if i:
                    wait_read(pe, l, "ds", i - 1)
                    heads((l, "ks", i), lambda q: c[:, 4 + q, tok_], lambda q: S[:, q, :])
                pe.wait_ge(sems["r_ready"], V("r_ready", l, i))
                wait_read(pe, l, "lx1", i, 2)
                heads((l, "u", i), lambda q: XT[:, q, :], lambda q: R[:, q, :])
                wait_read(pe, l, "qk", i)
                wait_read(pe, l, "u", i)
                if i:
                    pe.wait_ge(sems["qe_ready"], V("qe_ready", l))
                open_bank(pe, l, "oc", i)
                for q in range(CH):
                    o_ = bank(l, "oc", i)[:, P * q:P * q + P]
                    last = mm(o_, U[:, q, :], QK[:, q, :], start=True, stop=(i == 0))
                    if i:
                        last = mm(o_, S[:, q, :], qe[:, q, :], start=False, stop=True)
                last.then_inc(full(l, "oc", i), 1)
                turned("kt", 4)
                wait_read(pe, l, "kt", i)
                heads((l, "ds", i), lambda q: kd[:, q, :], lambda q: U[:, q, :])

            def gdn_s(l):
                pe.wait_ge(s0_in, 16 * (l + 1))
                open_bank(pe, l, "skq")
                for b in range(NS):
                    for q in range(CH):
                        n = CH * b + q
                        last = mm(bank(l, "skq")[:, 2 * n:2 * n + 2], S0[:, n, :], c[:, q:q + 5:4, NP_TOK + b],
                                  start=True, stop=True)
                last.then_inc(full(l, "skq"), 1)
                open_bank(pe, l, "sqk")
                pe.wait_ge(sems["gs_prod"], V("gs_prod", l))
                mm(bank(l, "sqk")[:, 0:32], ones, s_t, start=True, stop=True).then_inc(full(l, "sqk"), 1)
                open_bank(pe, l, "sgb")
                pe.wait_ge(sems["gs_d"], V("gs_d", l))
                mm(bank(l, "sgb")[:, 0:64], ones[0:NS, :], s_d, start=True, stop=True).then_inc(full(l, "sgb"), 1)
                open_bank(pe, l, "suk")
                pe.wait_ge(sems["gs_o"], V("gs_o", l))
                turn_over(bank(l, "suk")[0:32, 0:P], s_u, P)
                turn_over(bank(l, "suk")[0:32, P:2 * P], s_k, P).then_inc(full(l, "suk"), 1)
                wait_read(pe, l, "suk")
                for n in range(8):
                    if n % 2 == 0:
                        pe.wait_ge(sems["um_ready"], V("um_ready", l, n // 2))
                    open_bank(pe, l, "su", n)
                    mm(bank(l, "su", n), uk_sb[:, P:2 * P], um[n // 2 % 2][:, 4 * (n % 2):4 * (n % 2) + 4, :],
                       start=True, stop=True).then_inc(full(l, "su", n), 1)

            def gla_la(l):
                pe.wait_ge(wlr_in, 16 * (l + 1))
                wait_read(pe, l, "lr")
                for t in range(2):
                    open_bank(pe, l, "la", t)
                    mm(bank(l, "la", t)[:, 0:T], wlr[:, P * t:P * t + P], lr, start=True, stop=True).then_inc(
                        full(l, "la", t), 1)

            def gla_prep(l):
                wait_z(pe, l, Z_BV, Z_BG)
                for i in range(TT):
                    open_bank(pe, l, "vb", i)
                    for q in range(BH):
                        last = turn_over(bank(l, "vb", i)[:, P * q:P * q + P], z[:, Z_BV + q, P * i:P * i + P], P)
                    last.then_inc(full(l, "vb", i), 1)
                pe.wait_ge(sems["ke_ready"], V("ke_ready", l))
                open_bank(pe, l, "ket")
                for i in range(TT):
                    for t in range(2):
                        last = turn_over(bank(l, "ket")[:, P * (2 * i + t):P * (2 * i + t) + P],
                                         keg[:, t, P * i:P * i + P], P)
                last.then_inc(full(l, "ket"), 1)

            def gla_at(l, i):
                tok_ = slice(P * i, P * i + P)
                open_bank(pe, l, "ga", i)
                for q in range(BH):
                    last = mm(bank(l, "ga", i)[:, P * q:P * q + P], keg[:, q // 2, tok_], qz[:, q, tok_],
                              start=True, stop=True)
                last.then_inc(full(l, "ga", i), 1)
                wait_read(pe, l, "vb", i)
                wait_read(pe, l, "ga", i)
                open_bank(pe, l, "go", i)
                for q in range(BH):
                    last = mm(bank(l, "go", i)[:, P * q:P * q + P], vb[:, i, P * q:P * q + P], gatt[:, q, :],
                              start=True, stop=True)
                last.then_inc(full(l, "go", i), 1)

            def gla_ch(l, n):
                i, rows, cols = n // 2, slice(64 * (n % 2), 64 * (n % 2) + 64), slice(BC * n, BC * n + BC)
                if n:
                    pe.wait_ge(sems["gla_state"], V("gla_state", l, n - 1))
                    open_bank(pe, l, "gi", n)
                    for q in range(BH):
                        last = mm(bank(l, "gi", n)[:, 64 * q:64 * q + 64], GS[:, q // 2, :], qz[:, q, cols],
                                  start=True, stop=True)
                    last.then_inc(full(l, "gi", n), 1)
                wait_read(pe, l, "ket")
                open_bank(pe, l, "gs", n)
                for q in range(BH):
                    half = slice(64 * (q % 2), 64 * (q % 2) + 64)
                    last = mm(bank(l, "gs", n)[half, P * (q // 2):P * (q // 2) + P], ket[rows, i, 64 * q:64 * q + 64],
                              vb[rows, i, P * q:P * q + P], start=True, stop=True)
                last.then_inc(full(l, "gs", n), 1)

            def gla_s(l):
                open_bank(pe, l, "gk")
                for t in range(2):
                    last = turn_over(bank(l, "gk")[0:NS, P * t:P * t + P], z[:, Z_BK + t, NP_TOK:T], P)
                last.then_inc(full(l, "gk"), 1)
                open_bank(pe, l, "gv")
                for q in range(BH):
                    last = turn_over(bank(l, "gv")[0:NS, P * q:P * q + P], z[:, Z_BV + q, NP_TOK:T], P)
                last.then_inc(full(l, "gv"), 1)
                wait_read(pe, l, "gk")
                for n in range(4):
                    open_bank(pe, l, "gu", n)
                    for w in range(2):
                        q = 2 * (n // 2) + w
                        pe.wait_ge(sems["vm_ready"], V("vm_ready", l, q))
                        last = mm(bank(l, "gu", n)[64 * w:64 * w + 64, :], g_k[:, 64 * q:64 * q + 64],
                                  vm[w][:, 4 * (n % 2):4 * (n % 2) + 4, :], start=True, stop=True)
                    last.then_inc(full(l, "gu", n), 1)
                for n in range(4):
                    wait_read(pe, l, "gu", n)
                for w in range(2):
                    open_bank(pe, l, "gq", w)
                    half = slice(64 * w, 64 * w + 64)
                    for t in range(2):
                        for b in range(NS):
                            last = mm(bank(l, "gq", w)[:, 8 * t + b:8 * t + b + 1], g_s0[half, t, b, :],
                                      z[half, Z_BQ + t, NP_TOK + b:NP_TOK + b + 1], start=True, stop=True)
                    last.then_inc(full(l, "gq", w), 1)

            def kv_tok(l):
                pe.wait_ge(sems["n4_done"], V("n4_done", l, 9))
                wait_z(pe, l, Z_V, Z_G)
                for i in range(TT):
                    for n in range(6):
                        open_bank(pe, l, "tk", i, n)
                        base = Z_K + 4 * n
                        for t in range(4):
                            last = turn_over(bank(l, "tk", i, n)[:, P * t:P * t + P], z[:, base + t, P * i:P * i + P], P)
                        last.then_inc(full(l, "tk", i, n), 1)

            def att(l, q):
                half, t = slice(64 * (q % 2), 64 * (q % 2) + 64), q // 2

                def scores(i, g, out):
                    return mm(out, z[half, Z_Q + 4 * g + t, P * i:P * i + P], z[half, Z_K + 4 * g + t, 0:P * (i + 1)],
                              start=True, stop=True)

                for i in range(TT):
                    w = P * (i + 1)
                    open_bank(pe, l, "sc", q, i, 0)
                    for g in range(NG - i):
                        last = scores(i, g, bank(l, "sc", q, i, 0)[:, w * g:w * g + w])
                    last.then_inc(full(l, "sc", q, i, 0), 1)
                    if i:
                        open_bank(pe, l, "sc", q, i, 1)
                        scores(i, 2, bank(l, "sc", q, i, 1)[:, 0:w]).then_inc(full(l, "sc", q, i, 1), 1)
                    pe.wait_ge(sems["p_ready"], V("p_ready", l, 2 * q + i))
                    nb = NG * (i + 1)
                    for r in range(1 + i):
                        open_bank(pe, l, "pt", q, i, r)
                        for n in range(4 * r, min(4 * r + 4, nb)):
                            last = turn_over(bank(l, "pt", q, i, r)[:, P * (n % 4):P * (n % 4) + P],
                                             sc[i][:, P * n:P * n + P], P)
                        last.then_inc(full(l, "pt", q, i, r), 1)
                    open_bank(pe, l, "pv", q, i)
                    for r in range(1 + i):
                        wait_read(pe, l, "pt", q, i, r)
                    if q == 0:
                        for n in range(3, 6):
                            wait_read(pe, l, "tk", i, n)
                    for n in range(nb):
                        g, kt = n // (i + 1), n % (i + 1)
                        last = mm(bank(l, "pv", q, i)[:, 0:DH], pt[i][:, P * n:P * n + P],
                                  vtok[:, kt, 512 * g + DH * q:512 * g + DH * q + DH], start=(n == 0), stop=(n == nb - 1))
                    last.then_inc(full(l, "pv", q, i), 1)
                if q == AH - 1:
                    for i in range(TT):
                        wait_read(pe, l, "pv", q, i)
                        open_bank(pe, l, "oa", i)
                        for t_ in range(4):
                            last = turn_over(bank(l, "oa", i)[:, P * t_:P * t_ + P], oat[:, i, P * t_:P * t_ + P], P)
                        last.then_inc(full(l, "oa", i), 1)

            def att_s(l):
                for n in range(9):
                    open_bank(pe, l, "ts", n)
                    for t in range(4):
                        last = turn_over(bank(l, "ts", n)[0:NS, P * t:P * t + P], z[:, Z_Q + 4 * n + t, NP_TOK:T], P)
                    last.then_inc(full(l, "ts", n), 1)
                for n in range(NG):
                    wait_read(pe, l, "ts", n)
                for n in range(NG * NS):
                    g, b = n // NS, n % NS
                    open_bank(pe, l, "qb", n)
                    mm(bank(l, "qb", n), ident[0:NS, b:b + 1].to_broadcast([NS, P]), tok_g[:, 0, g, :],
                       start=True, stop=True).then_inc(full(l, "qb", n), 1)
                pe.wait_ge(sems["ls_ready"], V("ls_ready", l))
                open_bank(pe, l, "sx")
                mm(bank(l, "sx")[0:64, 0:24], K("esel", NS), sself, start=True, stop=True).then_inc(full(l, "sx"), 1)
                pe.wait_ge(sems["l_ready"], V("l_ready", l))
                open_bank(pe, l, "lt")
                for g in range(NG):
                    last = turn_over(bank(l, "lt")[0:64, P * g:P * g + P], L[:, 64 * g:64 * g + 64], P)
                last.then_inc(full(l, "lt"), 1)
                pe.wait_ge(sems["ps_ready"], V("ps_ready", l))
                open_bank(pe, l, "pk")
                for g in range(NG):
                    last = turn_over(bank(l, "pk")[:, 64 * g:64 * g + 64], sp_[:, P * g:P * g + P], 64)
                last.then_inc(full(l, "pk"), 1)
                pe.wait_ge(sems["dd_ready"], V("dd_ready", l))
                open_bank(pe, l, "rr")
                for t in range(4):
                    last = mm(bank(l, "rr")[:, 32 * t:32 * t + 32], K("hmap", 64)[:, P * t:P * t + P],
                              dd.rearrange("p a b -> p (a b)"), start=True, stop=True)
                last.then_inc(full(l, "rr"), 1)
                wait_read(pe, l, "pk")
                open_bank(pe, l, "pvs")
                for b in range(NS):
                    for g in range(NG):
                        n = 24 + NG * b + g
                        pe.wait_ge(cache_in[n % 6], 16 * (8 * l + n // 6 + 1))
                    for q in range(AH):
                        for g in range(NG):
                            last = mm(bank(l, "pvs")[64 * (q % 2):64 * (q % 2) + 64, 8 * (q // 2) + b:8 * (q // 2) + b + 1],
                                      cache[(24 + NG * b + g) % 6][:, DH * q:DH * q + DH],
                                      pts[:, 64 * g + 8 * b + q:64 * g + 8 * b + q + 1],
                                      start=(g == 0), stop=(g == NG - 1))
                    if b < NS - 1:
                        last.then_inc(sems["v_used"], 1)
                last.then_inc(full(l, "pvs"), 1)

            def merge(l):
                src = [oaT, z[:, Z_BG:Z_BG + 4, :], z[:, Z_CZ:Z_CZ + 4, :]]
                pe.wait_ge(sems["oas_ready"], V("oas_ready", l))
                pe.wait_ge(sems["n4_done"], V("n4_done", l, 9))
                for b in range(3):
                    ch = [CH0[l] + CH_PROJ + 2 * b + q for q in range(2)]
                    for n in ch:
                        wait_chunk(pe, n)
                    for d in range(KT):
                        open_bank(pe, l, "mb", b, d)
                        for k in range(4):
                            last = mm(bank(l, "mb", b, d)[:, 0:T],
                                      v3(chunk(ch[k // 2]), 2)[:, k % 2, P * d:P * d + P], src[b][:, k, :],
                                      start=(k == 0), stop=(k == 3))
                        last.then_inc(full(l, "mb", b, d), 1)
                pe.wait_ge(sems["acc_ready"], V("acc_ready", l))
                for d in range(KT):
                    n = CH0[l] + CH_PROJ + CH_WB + d // 2
                    if d % 2 == 0:
                        wait_chunk(pe, n)
                    open_bank(pe, l, "wo", d)
                    w = v3(chunk(n), KT)
                    for k in range(KT):
                        last = mm(bank(l, "wo", d)[:, 0:T], w[:, k, P * (d % 2):P * (d % 2) + P], z[:, k, :],
                                  start=(k == 0), stop=(k == KT - 1))
                    last.then_inc(full(l, "wo", d), 1)

            def ffn0():
                pe.wait_ge(sems["h_ready"], V("h_ready", 0, 1))
                for i in range(FF // P):
                    for w_, name in enumerate(("fg", "fu")):
                        n = CH_MIX + 2 * (i // 2) + w_
                        if i % 2 == 0:
                            wait_chunk(pe, n)
                        open_bank(pe, 0, name, i)
                        w = v3(chunk(n), KT)
                        dense((0, name, i), lambda k: w[:, k, P * (i % 2):P * (i % 2) + P], 0)
                for q in range(CH_FFD):
                    n = CH_MIX + CH_FFG + q
                    wait_chunk(pe, n)
                    for w_ in range(2):
                        k = 2 * q + w_
                        wait_read(pe, 0, "fu", k)
                        for d in range(KT):
                            if k == 0:
                                open_bank(pe, 0, "fd", d)
                            last = mm(bank(0, "fd", d)[:, 0:T], v3(chunk(n), 2)[:, w_, P * d:P * d + P], fa[:, k, :],
                                      start=(k == 0), stop=(k == FF // P - 1))
                            if k == FF // P - 1:
                                last.then_inc(full(0, "fd", d), 1)
                    if q < CH_FFD - 1:
                        last.then_inc(down_used, 1)

            def route():
                pe.wait_ge(sems["h_ready"], V("h_ready", 1, 1))
                pe.wait_ge(router_in, 16)
                open_bank(pe, 1, "rl", 0)
                for k in range(KT):
                    last = mm(bank(1, "rl", 0)[0:NE, 0:T], wr[:, 8 * k:8 * k + 8], h[:, k, :],
                              start=(k == 0), stop=(k == KT - 1))
                last.then_inc(full(1, "rl", 0), 1)
                wait_read(pe, 1, "rl", 0)
                open_bank(pe, 1, "rt", 0)
                for i, (t0, nt) in enumerate(TOKS):
                    last = turn_over(bank(1, "rt", 0)[0:nt, 8 * i:8 * i + 8], rlog[0:NE, t0:t0 + nt], NE)
                last.then_inc(full(1, "rt", 0), 1)
                pe.wait_ge(r_gate, 1)
                open_bank(pe, 1, "gt", 0)
                for i, (t0, nt) in enumerate(TOKS):
                    last = turn_over(bank(1, "gt", 0)[0:NE, t0:t0 + nt], rg[0:nt, i, :], nt)
                last.then_inc(full(1, "gt", 0), 1)
                pe.wait_ge(r_mask, 1)
                open_bank(pe, 1, "rp", 0)
                b_ = bank(1, "rp", 0)
                for i, (_, nt) in enumerate(TOKS):
                    for j in range(i):
                        mm(b_[0:nt, 8 * i:8 * i + 8], ones[:, 0:nt], rmask[:, j, :], start=(j == 0), stop=False)
                    mm(b_[0:nt, 8 * i:8 * i + 8], K("upper")[0:nt, 0:nt], rmask[0:nt, i, :], start=(i == 0), stop=True)
                for i, (_, nt) in enumerate(TOKS):
                    last = mm(b_[:, 24:32], ones[0:nt, :], rmask[0:nt, i, :], start=(i == 0), stop=(i == 2))
                last.then_inc(full(1, "rp", 0), 1)
                for n in range(2 * len(TOKS)):
                    t0, nt = TOKS[n // 2]
                    open_bank(pe, 1, "ht", n)
                    for k in range(4):
                        last = turn_over(bank(1, "ht", n)[0:nt, P * k:P * k + P], h[:, 4 * (n % 2) + k, t0:t0 + nt], P)
                    last.then_inc(full(1, "ht", n), 1)
                for e in range(NE):
                    pe.wait_ge(r_back, e + 1)
                    open_bank(pe, 1, "st", e)
                    for i, (t0, nt) in enumerate(TOKS):
                        last = turn_over(bank(1, "st", e)[:, t0:t0 + nt], gw[e % 2][0:nt, i, :], nt)
                    last.then_inc(full(1, "st", e), 1)
                pe.wait_ge(r_gate, 2)
                pe.wait_ge(r_slots, 1)
                for e in range(NE):
                    wait_read(pe, 1, "st", e)
                for n in range(2 * len(TOKS)):
                    wait_read(pe, 1, "ht", n)

            def landed_e(e, q):
                s_ = q % RING_F
                pe.wait_ge(landed[s_], e * (16 * N_EXP_CH // RING_F) + 16 * (moe_loads[s_] + q // RING_F + 1))

            def hidden(e, src, n):
                for i in range(FE // P):
                    for w_, name in enumerate(("fg", "fu")):
                        q = 2 * (i // 2) + w_
                        if i % 2 == 0:
                            landed_e(e, q)
                        open_bank(pe, 1, name, i, e=e)
                        w = v3(slot_ap(q % RING_F), KT)
                        for k in range(KT):
                            last = mm(bank(1, name, i)[:, 0:n], w[:, k, P * (i % 2):P * (i % 2) + P], src[:, k, :],
                                      start=(k == 0), stop=(k == KT - 1))
                        last.then_inc(full(1, name, i), 1)

            def experts_all():
                with pe.Fori(0, NE) as e:
                    open_bank(pe, 1, "gh", 0, e=e)
                    pe.wait_ge(r_gate, 2)
                    mm(bank(1, "gh", 0)[:, 0:T], ones[0:NE, :], g8[:, bass.ds(e, 1), :].rearrange("p a b -> p (a b)"),
                       start=True, stop=True).then_inc(full(1, "gh", 0), 1)
                    open_bank(pe, 1, "gh", 1, e=e)
                    mm(bank(1, "gh", 1)[:, 0:8], ones, ones[:, 0:8], start=True, stop=True).then_inc(
                        full(1, "gh", 1), 1)
                    hidden(e, h, T)
                    for w_ in range(2):
                        open_bank(pe, 1, "dn", w_, e=e)
                        mm(bank(1, "dn", w_)[:, 0:8], ones, ones[:, 0:8], start=True, stop=True).then_inc(
                            full(1, "dn", w_), 1)
                    for q in range(CH_ED):
                        landed_e(e, CH_EG + q)
                        w = v3(slot_ap((CH_EG + q) % RING_F), 2)
                        for w_ in range(2):
                            k = 2 * q + w_
                            wait_read(pe, 1, "fu", k, e=e)
                            for d in range(KT):
                                if k == 0:
                                    open_bank(pe, 1, "fd", d, e=e)
                                last = mm(bank(1, "fd", d)[:, 0:T], w[:, w_, P * d:P * d + P], fa[:, k, :],
                                          start=(k == 0), stop=(k == FE // P - 1))
                                if k == FE // P - 1:
                                    last.then_inc(full(1, "fd", d), 1)
                        if q < CH_ED - 1:
                            last.then_inc(down_used, 1)

            def experts_chosen():
                with pe.Fori(0, NE) as e:
                    for w_ in range(2):
                        open_bank(pe, 1, "gh", w_, e=e)
                        for k in range(4):
                            for i, (_, nt) in enumerate(TOKS):
                                last = mm(bank(1, "gh", w_)[:, P * k:P * k + P],
                                          htok[0:nt, i, P * (4 * w_ + k):P * (4 * w_ + k) + P],
                                          G[0:nt, i, bass.ds(e, 1), :].rearrange("p a b -> p (a b)"),
                                          start=(i == 0), stop=(i == 2))
                        last.then_inc(full(1, "gh", w_), 1)
                    for w_ in range(2):
                        wait_read(pe, 1, "gh", w_, e=e)
                    hidden(e, hs, P)
                    for w_ in range(2):
                        open_bank(pe, 1, "dn", w_, e=e)
                    for q in range(CH_ED):
                        landed_e(e, CH_EG + q)
                        w = v3(slot_ap((CH_EG + q) % RING_F), 2)
                        for w_ in range(2):
                            k = 2 * q + w_
                            wait_read(pe, 1, "fu", k, e=e)
                            for n in range(2):
                                last = mm(bank(1, "dn", n), fa[:, k, 0:P], w[:, w_, 512 * n:512 * n + 512],
                                          start=(k == 0), stop=(k == FE // P - 1))
                                if k == FE // P - 1:
                                    last.then_inc(full(1, "dn", n), 1)
                        if q < CH_ED - 1:
                            last.then_inc(down_used, 1)
                    for d in range(KT):
                        wait_read(pe, 1, "dn", d // 4, e=e)
                        open_bank(pe, 1, "fd", d, e=e)
                        mm(bank(1, "fd", d)[:, 0:T], ys[:, P * d:P * d + P],
                           ST[:, bass.ds(e, 1), :].rearrange("p a b -> p (a b)"), start=True, stop=True).then_inc(
                            full(1, "fd", d), 1)

            def experts():
                pe.wait_ge(r_flag, 1)
                many = pe.value_load(crowded[0:1, 0:1], min_val=0, max_val=1)
                with pe.If(many):
                    experts_all()
                with pe.Else():
                    experts_chosen()

            pe.wait_ge(con_in, 16)
            pe.wait_ge(x_in, 48)
            for k in range(KT):
                open_bank(pe, "x0", k)
                for i, (t0, nt) in enumerate(TOKS):
                    last = turn_over(bank("x0", k)[:, t0:t0 + nt], xst[i][0:nt, P * k:P * k + P], nt)
                last.then_inc(full("x0", k), 1)
            pe.wait_ge(setup_in, 16)
            pe.wait_ge(relb_in, 16)
            pe.wait_ge(relb_one, 1)
            for n in range(24):
                open_bank(pe, "tab", n)
                mm(bank("tab", n), relb[:, n:n + 1].to_broadcast([NB + 1, P]),
                   setup[:, S_TAB + 512 * (n // AH):S_TAB + 512 * (n // AH) + 512], start=True, stop=True).then_inc(
                    full("tab", n), 1)
            open_bank(pe, "bs")
            for g in range(NG):
                last = mm(bank("bs")[:, 8 * g:8 * g + 8], setup[0:NB, S_KEY + P * g:S_KEY + P * g + P],
                          relb[0:NB, 8 * g:8 * g + 8], start=True, stop=True)
            last.then_inc(full("bs"), 1)
            open_bank(pe, "bself")
            mm(bank("bself")[0:NS, 0:24], setup[0:NB, S_SELF:S_SELF + NS], relb[0:NB, 0:24],
               start=True, stop=True).then_inc(full("bself"), 1)
            run = dict(small=small_step, proj=proj, conv=conv, gate_c=gate_c, norm4=norm4, gdn_dec=gdn_dec, gdn_a=gdn_a,
                       gdn_sq=gdn_sq, gdn_lv=gdn_lv, gdn_st=gdn_st, gdn_s=gdn_s, gla_la=gla_la, gla_prep=gla_prep,
                       gla_at=gla_at, gla_ch=gla_ch, gla_s=gla_s, kv_tok=kv_tok, att=att, att_s=att_s,
                       merge=merge, xnorm=xnorm)
            for l in range(DEPTH):
                for step in SCHED[l]:
                    if step[0] in run:
                        run[step[0]](l, *step[1:])
                xnorm(l, 1)
                if l == 0:
                    ffn0()
                else:
                    route()
                    experts()
            for k in range(KT):
                wait_read(pe, 1, "fd", k, e=NE - 1)
            for n in range(2 * len(TOKS)):
                t0, nt = TOKS[n // 2]
                open_bank(pe, "y", n)
                for k in range(4):
                    last = turn_over(bank("y", n)[0:nt, P * k:P * k + P], x[:, 4 * (n % 2) + k, t0:t0 + nt], P)
                last.then_inc(full("y", n), 1)

        @block.scalar
        def _(act):
            steps = [0]

            def link(ins):
                steps[0] += 1
                ins.then_inc(act_s, 1)
                act.wait_ge(act_s, steps[0])

            def settle():
                steps[0] += 1
                act.drain().then_inc(act_s, 1)
                act.wait_ge(act_s, steps[0])

            def act_(out, in_, func, **kw):
                return nc.scalar.activation(out, in_, func, **kw)

            def copy(out, in_):
                return nc.scalar.copy(out, in_)

            copies = [(g, l, b) for l in range(DEPTH) for b in range(NS) for g in (2, 1, 0)]

            def shift_cache(g, l, b):
                name, win = CACHES[g]
                act.dma_start(o[f"win{win}_s"][l][b].rearrange("w k h d -> (w k h d)")[0:(win - 1) * 1024],
                              a[name][l][b].rearrange("w k h d -> (w k h d)")[1024:win * 1024]).then_inc(stored["copy"], 16)

            def xnorm(l, w):
                if l or w:
                    for d in range(KT):
                        wait_read(act, l if w else 0, *(("wo", d) if w else ("fd", d)))
                else:
                    for k in range(KT):
                        wait_read(act, "x0", k)
                act_(z[:, 0:KT, :], x[:, :, :], ACT.Square).then_inc(sems["sq_ready"], 1)
                wait_full(act, l, "xn", w)
                act_(rs, bank(l, "xn", w)[:, 0:T], ACT.Ln, scale=1.0 / D, bias=epsc).then_inc(free(l, "xn", w), 1)
                wait_read(act, l, "xn", w)
                act_(rs, rs, ACT.Exp, scale=-0.5).then_inc(sems["rs_ready"], 1)

            def proj(l, j):
                if l == 0 and j == 40:
                    act.wait_ge(tab_out[0], 16)
                wait_full(act, l, "p", j)
                copy(z[:, j, :], bank(l, "p", j)[:, 0:T]).then_inc(free(l, "p", j), 1)
                if j % 4 == 1 and copies:
                    shift_cache(*copies.pop(0))

            def small_step(l):
                act.wait_ge(sems["xa_ready"], V("xa_ready", l))
                link(act_(gl, gabs, ACT.Exp, scale=-1.0))
                act_(gl, gl, ACT.Ln, bias=1.0)
                act_(ealog, ab[:, 0:4], ACT.Exp).then_inc(sems["g_exp"], 1)

            def conv(l):
                act.wait_ge(sems["conv_sum"], V("conv_sum", l))
                for q in range(3):
                    wait_read(act, l, "co", q)
                act_(beta, cba[:, :, 0:4], ACT.Sigmoid)
                act_(z[:, 0:12, :], c[:, :, :], ACT.Sigmoid).then_inc(sems["conv_sig"], 1)
                act.wait_ge(sems["conv_done"], V("conv_done", l))
                wait_z(act, l, Z_CZ, Z_BQ)
                act_(z[:, 8:12, :], z[:, Z_CZ:Z_CZ + 4, :], ACT.Sigmoid).then_inc(sems["cz_sig"], 1)

            def gate_c(l):
                act.wait_ge(sems["btok_ready"], V("btok_ready", l))
                link(act_(ebtok, btok, ACT.Exp))
                nc.scalar.mul(nebtok, ebtok, -1.0)

            def norm4(l, n):
                buf, base, _, scale, _w = N4[n]
                if n >= 2 and n != 4:
                    act.wait_ge(sems["n4_done"], V("n4_done", l, n - 2))
                if n in (0, 1):
                    act.wait_ge(sems["conv_done"], V("conv_done", l))
                    act.wait_ge(sems["cz_done"], V("cz_done", l))
                elif n == 2:
                    act.wait_ge(sems["s_o"], V("s_o", l))
                elif n == 3:
                    wait_read(act, l, "gi", 3)
                    wait_read(act, l, "gq", 1)
                else:
                    act.wait_ge(sems["n4_done"], V("n4_done", l, n - 2))
                    wait_z(act, l, base, base + 4)
                act_(sq4(n), buf[:, base:base + 4, :], ACT.Square).then_inc(sems["sq4"], 1)
                for t in range(4):
                    wait_full(act, l, "n4", n, t)
                    act_(sq4(n)[:, t, :], bank(l, "n4", n, t)[:, 0:T], ACT.Ln, scale=scale, bias=epsc).then_inc(
                        free(l, "n4", n, t), 1)
                for t in range(4):
                    wait_read(act, l, "n4", n, t)
                act_(sq4(n), sq4(n), ACT.Exp, scale=-0.5).then_inc(sems["rs4"], 1)

            def gdn_dec(l, i):
                if i:
                    wait_read(act, l, "ds", i - 1)
                wait_full(act, l, "brow", i)
                act_(ebr, v3(bank(l, "brow", i), 4), ACT.Exp).then_inc(sems["ebr_ready"], 1)
                act.wait_ge(sems["t1_ready"], V("t1_ready", l, i))
                for q in range(CH):
                    n = 4 * i + q
                    act_(QK[:, q, :], t1[:, q, :], ACT.Exp, bias=nbtok[:, n:n + 1])
                    last = act_(A[:, q, :], R[:, q, :], ACT.Exp, scale=-1.0, bias=btok[:, n:n + 1])
                last.then_inc(sems["dec_ready"], 1)

            def gdn_a(l, i):
                wait_full(act, l, "at", i)
                copy(AT, v3(bank(l, "at", i), 4)).then_inc(free(l, "at", i), 1)

            def gdn_sq(l, i, q):
                wait_full(act, l, "sq0", i, q)
                if q < 2:
                    wait_full(act, l, "sq1", i, q)
                copy(Pm, v3(bank(l, "sq0", i, q), 4)).then_inc(free(l, "sq0", i, q), 1)

            def gdn_lv(l, i, v):
                wait_full(act, l, "y", i, v)
                copy(Y, v3(bank(l, "y", i, v), 4)).then_inc(free(l, "y", i, v), 1)

            def gdn_st(l, i):
                wait_full(act, l, "vt", i)
                copy(R, v3(bank(l, "vt", i), 4)).then_inc(free(l, "vt", i), 1)
                wait_full(act, l, "u", i)
                copy(U, v3(bank(l, "u", i), 4)).then_inc(free(l, "u", i), 1)
                act.wait_ge(sems["dlx_ready"], V("dlx_ready", l, i))
                act_(dl, dl, ACT.Exp).then_inc(sems["dl_ready"], 1)
                wait_full(act, l, "oc", i)
                copy(c[:, 8:12, P * i:P * i + P], v3(bank(l, "oc", i), 4)).then_inc(free(l, "oc", i), 1)

            def gdn_s(l):
                act.wait_ge(sems["gs_k"], V("gs_k", l))
                act_(s_eg[0:NS], gl[0:NS, 2, :], ACT.Exp).then_inc(sems["gs_eg"], 1)
                wait_full(act, l, "suk")
                copy(uk_sb, bank(l, "suk")[0:32, 0:256]).then_inc(free(l, "suk"), 1)

            def gla_la(l):
                wait_z(act, l, Z_BG, Z_Q)
                act_(z[:, 8:12, :], z[:, Z_BG:Z_BG + 4, :], ACT.Sigmoid).then_inc(sems["bg_sig"], 1)
                act.wait_ge(sems["la_x"], V("la_x", l))
                link(act_(laa, laa, ACT.Exp, scale=-1.0))
                act_(laa, laa, ACT.Ln, bias=1.0).then_inc(sems["la_e"], 1)
                act.wait_ge(sems["b_ready"], V("b_ready", l))
                act_(geb, gb, ACT.Exp)
                act_(keg, gb, ACT.Exp, scale=-1.0)
                act_(g_a.rearrange("p (q b) -> p q b", q=2), la[:, :, NP_TOK:T], ACT.Exp).then_inc(sems["eb_ready"], 1)

            def gla_prep(l):
                for i in range(TT):
                    wait_full(act, l, "vb", i)
                    copy(vb[:, i, :], bank(l, "vb", i)).then_inc(free(l, "vb", i), 1)
                wait_full(act, l, "ket")
                copy(ket, v3(bank(l, "ket"), 2)).then_inc(free(l, "ket"), 1)

            def gla_at(l, i):
                wait_full(act, l, "go", i)
                copy(ob[:, :, P * i:P * i + P], v3(bank(l, "go", i), 4)).then_inc(free(l, "go", i), 1)

            def gla_s(l):
                wait_full(act, l, "gk")
                copy(g_k, bank(l, "gk")[0:NS, 0:256]).then_inc(free(l, "gk"), 1)
                wait_full(act, l, "gv")
                copy(g_v, bank(l, "gv")[0:NS, :]).then_inc(free(l, "gv"), 1)

            def kv_tok(l):
                for i in range(TT):
                    for n in range(3, 6):
                        wait_full(act, l, "tk", i, n)
                        copy(vtok[:, i, 512 * (n - 3):512 * (n - 2)], bank(l, "tk", i, n)).then_inc(
                            free(l, "tk", i, n), 1)

            def att(l, q):
                for i in range(TT):
                    u = 2 * q + i
                    w = NG * P * (i + 1)
                    act.wait_ge(sems["sc_add"], V("sc_add", l, u))
                    act_(sc[i][:, 0:w], sc[i][:, 0:w], ACT.Exp, bias=rowmax[:, u:u + 1],
                         accum_out=rowsum[:, u:u + 1]).then_inc(sems["p_ready"], 1)
                    for r in range(1 + i):
                        wait_full(act, l, "pt", q, i, r)
                        n = min(512, w - 512 * r)
                        copy(pt[i][:, 512 * r:512 * r + n], bank(l, "pt", q, i, r)[:, 0:n]).then_inc(
                            free(l, "pt", q, i, r), 1)
                if q == AH - 1:
                    for i in range(TT):
                        wait_full(act, l, "oa", i)
                        copy(oaT[:, :, P * i:P * i + P], v3(bank(l, "oa", i), 4)).then_inc(free(l, "oa", i), 1)

            def att_s(l):
                for n in range(9):
                    wait_full(act, l, "ts", n)
                    copy(tok[:, 512 * n:512 * n + 512], bank(l, "ts", n)[0:NS, :]).then_inc(free(l, "ts", n), 1)
                act.wait_ge(sems["sp_max"], V("sp_max", l))
                act_(sp_, sp_, ACT.Exp, bias=rowmax[0:64, 0:1], accum_out=rowsum[0:64, 0:1]).then_inc(sems["ps_ready"], 1)
                wait_full(act, l, "pk")
                copy(pts, bank(l, "pk")[:, 0:192]).then_inc(free(l, "pk"), 1)

            def sig(l):
                wait_z(act, l, Z_G, Z_N)
                for b in range(3):
                    last = act_(z[:, Z_G + 8 * b:Z_G + 8 * b + 8, :], z[:, Z_G + 8 * b:Z_G + 8 * b + 8, :], ACT.Sigmoid)
                last.then_inc(sems["sig_ready"], 1)

            def bar(l, n):
                act.drain().then_inc(sems["bar_a"], 1)
                act.wait_ge(sems["bar_v"], V("bar_v", l, n))

            def hidden(l, i, e=None, n=T):
                wait_full(act, l, "fg", i, e=e)
                if i >= 4:
                    wait_read(act, l, "fu", i - 4, e=e)
                elif e is not None:
                    b_, m = JOB[(l, "fu", FE // P - 4 + i)]
                    act.wait_ge(bank_free[b_], e * moe_per[b_] + (m + 1 - moe_per[b_]))
                act_(fs[:, i % 4, 0:n], bank(l, "fg", i)[:, 0:n], ACT.Silu).then_inc(free(l, "fg", i), 1)

            act.dma_start(xst[0], a["x_prompt"][0, 0:P, :]).then_inc(x_in, 16)
            act.dma_start(xst[1], a["x_prompt"][0, P:2 * P, :]).then_inc(x_in, 16)
            act.dma_start(xst[2][0:NS, :], a["x_sample"].rearrange("b t d -> (b t) d")).then_inc(x_in, 16)
            for k in range(KT):
                wait_full(act, "x0", k)
                copy(x[:, k, :], bank("x0", k)[:, 0:T]).then_inc(free("x0", k), 1)
            for n in range(24):
                wait_full(act, "tab", n)
                copy(ztab[:, n, :], bank("tab", n)).then_inc(free("tab", n), 1)
            wait_full(act, "bs")
            copy(biask, bank("bs")[:, 0:24]).then_inc(free("bs"), 1)
            wait_full(act, "bself")
            copy(bself, bank("bself")[0:NS, 0:24]).then_inc(free("bself"), 1)
            for n in range(16, 24):
                wait_read(act, "tab", n)
            act.dma_start(dscr.rearrange("n p c -> p n c"), ztab).then_inc(tab_out[0], 16)
            run = dict(small=small_step, proj=proj, conv=conv, gate_c=gate_c, norm4=norm4, gdn_dec=gdn_dec, gdn_a=gdn_a,
                       gdn_sq=gdn_sq, gdn_lv=gdn_lv, gdn_st=gdn_st, gdn_s=gdn_s, gla_la=gla_la, gla_prep=gla_prep,
                       gla_at=gla_at, gla_s=gla_s, kv_tok=kv_tok, att=att, att_s=att_s, xnorm=xnorm, sig=sig,
                       bar=bar)
            for l in range(DEPTH):
                for step in SCHED[l]:
                    if step[0] in run:
                        if step[0] != "proj":
                            settle()
                        run[step[0]](l, *step[1:])
                settle()
                xnorm(l, 1)
                if l == 0:
                    for i in range(FF // P):
                        hidden(0, i)
                        if i % 4 == 1:
                            shift_cache(*copies.pop(0))
            assert not copies
            act.wait_ge(r_max, 1)
            act_(rexp, rexp, ACT.Exp).then_inc(r_exp, 1)
            for n in range(2 * len(TOKS)):
                nt = TOKS[n // 2][1]
                wait_full(act, 1, "ht", n)
                copy(htok[0:nt, n // 2, 512 * (n % 2):512 * (n % 2) + 512], bank(1, "ht", n)[0:nt, :]).then_inc(
                    free(1, "ht", n), 1)
            for e in range(NE):
                wait_full(act, 1, "st", e)
                copy(ST[:, e, :], bank(1, "st", e)[:, 0:T]).then_inc(free(1, "st", e), 1)

            def experts(chosen):
                with act.Fori(0, NE) as e:
                    if chosen:
                        for w_ in range(2):
                            wait_full(act, 1, "gh", w_, e=e)
                            copy(hs[:, 4 * w_:4 * w_ + 4, :], v3(bank(1, "gh", w_), 4)).then_inc(free(1, "gh", w_), 1)
                    for i in range(FE // P):
                        hidden(1, i, e=e, n=P if chosen else T)
                    for w_ in range(2):
                        wait_full(act, 1, "dn", w_, e=e)
                        n = 512 if chosen else 8
                        copy(ys[:, 512 * w_:512 * w_ + n], bank(1, "dn", w_)[:, 0:n]).then_inc(free(1, "dn", w_), 1)

            act.wait_ge(r_flag, 1)
            many = act.value_load(crowded[0:1, 0:1], min_val=0, max_val=1)
            with act.If(many):
                experts(False)
            with act.Else():
                experts(True)
            for n in range(2 * len(TOKS)):
                nt = TOKS[n // 2][1]
                wait_full(act, "y", n)
                copy(yst[n // 2][0:nt, 512 * (n % 2):512 * (n % 2) + 512], bank("y", n)[0:nt, :]).then_inc(
                    free("y", n), 1)
                if n % 2:
                    wait_read(act, "y", n - 1)
                    wait_read(act, "y", n)
                    dst = (o["y_prompt"][0, P * (n // 2):P * (n // 2) + P, :] if n < 4
                           else o["y_sample"].rearrange("b t d -> (b t) d"))
                    act.dma_start(dst, yst[n // 2][0:nt, :]).then_inc(stored["y"], 16)

        @block.vector
        def _(dve):
            steps = [0]
            tt, ts, stt, cp = (nc.vector.tensor_tensor, nc.vector.tensor_scalar, nc.vector.scalar_tensor_tensor,
                               nc.vector.tensor_copy)
            MUL, ADD, SUB, MAX = ALU.mult, ALU.add, ALU.subtract, ALU.max

            def link(ins):
                steps[0] += 1
                ins.then_inc(vec, 1)
                dve.wait_ge(vec, steps[0])

            def settle():
                steps[0] += 1
                dve.drain().then_inc(vec, 1)
                dve.wait_ge(vec, steps[0])

            def xnorm(l, w):
                if w == 0:
                    wait_full(dve, l, "par")
                    cp(par, bank(l, "par")[:, 0:R_N]).then_inc(free(l, "par"), 1)
                    wait_read(dve, l, "par")
                    link(ts(qnw, par[:, R_QN:R_QN + 1], float(DH) ** -0.5, None, MUL))
                dve.wait_ge(sems["rs_ready"], V("rs_ready", l, w))
                for k in range(KT):
                    r = (R_NF if w else R_NM) + k
                    last = stt(h[:, k, :], x[:, k, :], par[:, r:r + 1], rs, MUL, MUL)
                last.then_inc(sems["h_ready"], 1)

            def small_step(l):
                wait_full(dve, l, "ab")
                cp(ab, bank(l, "ab")[:, 0:8]).then_inc(free(l, "ab"), 1)
                wait_full(dve, l, "cba")
                cp(cba[:, 0:2, :], v3(bank(l, "cba")[:, 0:16], 2))
                cp(cba[0:NS, 2, :], bank(l, "cba")[0:NS, 16:24]).then_inc(free(l, "cba"), 1)
                wait_read(dve, l, "ab")
                wait_read(dve, l, "cba")
                link(tt(xa, cba[:, :, 4:8], bc(ab[:, 4:8], 1, [P, 3, 4]), ADD))
                stt(gabs, xa, -1.0, xa, MUL, MAX).then_inc(sems["xa_ready"], 1)
                wait_full(dve, l, "lr")
                cp(lr, bank(l, "lr")[0:BRANK, 0:T]).then_inc(free(l, "lr"), 1)
                dve.wait_ge(sems["g_exp"], V("g_exp", l))
                link(stt(xa, xa, 0.0, gl, MAX, ADD))
                stt(gl, xa, -1.0, bc(ealog, 1, [P, 3, 4]), MUL, MUL).then_inc(sems["g_ready"], 1)

            def conv(l):
                wait_z(dve, l, 0, 12)
                for k in range(CONVW - 1, -1, -1):
                    s_ = CONVW - 1 - k
                    for j in range(12):
                        w = par[:, R_CV + 12 * k + j:R_CV + 12 * k + j + 1]
                        if s_ == 0:
                            last = ts(c[:, j, 0:NP_TOK], z[:, j, 0:NP_TOK], w, None, MUL)
                        else:
                            last = stt(c[:, j, s_:NP_TOK], z[:, j, 0:NP_TOK - s_], w, c[:, j, s_:NP_TOK], MUL, ADD)
                    link(last)
                wait_full(dve, l, "cs")
                cp(catS[:, :, :, 0:3], bank(l, "cs")[:, 0:288].rearrange("p (j b k) -> p j b k", j=12, b=NS)).then_inc(
                    free(l, "cs"), 1)
                link(cp(catS[:, :, :, 3], z[:, 0:12, NP_TOK:T]))
                wait_read(dve, l, "cs")
                w = par[:, R_CV:R_CV + 48].rearrange("p (k j) -> p j k", k=CONVW)
                link(tt(catS, catS, bc(w, 2, [P, 12, NS, CONVW]), MUL))
                nc.vector.tensor_reduce(c[:, :, NP_TOK:T], catS, AX.X, ADD).then_inc(sems["conv_sum"], 1)
                for q in range(3):
                    wait_full(dve, l, "co", q)
                    cp(convt[0:11, 512 * q:512 * q + 512], bank(l, "co", q)[0:11, :]).then_inc(free(l, "co", q), 1)
                dve.wait_ge(sems["conv_sig"], V("conv_sig", l))
                tt(c[:, :, :], c[:, :, :], z[:, 0:12, :], MUL).then_inc(sems["conv_done"], 1)
                dve.wait_ge(sems["cz_sig"], V("cz_sig", l))
                tt(z[:, Z_CZ:Z_CZ + 4, :], z[:, Z_CZ:Z_CZ + 4, :], z[:, 8:12, :], MUL).then_inc(sems["cz_done"], 1)

            def gate_c(l):
                wait_full(dve, l, "btok")
                cp(btok, bank(l, "btok")[:, 0:8]).then_inc(free(l, "btok"), 1)
                wait_read(dve, l, "btok")
                ts(nbtok, btok, -1.0, None, MUL).then_inc(sems["btok_ready"], 1)

            def norm4(l, n):
                buf, base, _, _s, w = N4[n]
                dve.wait_ge(sems["rs4"], V("rs4", l, n))
                t_ = buf[:, base:base + 4, :]
                if n < 2:
                    stt(t_, t_, float(CD) ** -0.5 if n == 0 else 1.0, sq4(n), MUL, MUL).then_inc(sems["n4_done"], 1)
                elif n < 4:
                    link(stt(t_, t_, w, sq4(n), MUL, MUL))
                    g_ = z[:, Z_CZ:Z_CZ + 4, :] if n == 2 else z[:, Z_BG:Z_BG + 4, :]
                    tt(g_, g_, t_, MUL).then_inc(sems["n4_done"], 1)
                else:
                    stt(t_, t_, w, sq4(n), MUL, MUL).then_inc(sems["n4_done"], 1)

            def gdn_dec(l, i):
                wait_full(dve, l, "brow", i)
                b_ = v3(bank(l, "brow", i), 4)
                dve.wait_ge(sems["ebr_ready"], V("ebr_ready", l, i))
                tt(t1, b_, bc(K("neg_t"), 1, [P, 4, P]), ADD)
                tt(R, b_, bc(K("pos_s"), 1, [P, 4, P]), ADD).then_inc(sems["t1_ready"], 1)
                cp(blast, b_[:, :, P - 1]).then_inc(free(l, "brow", i), 1)

            def gdn_a(l, i):
                dve.wait_ge(sems["dec_ready"], V("dec_ready", l, i))
                wait_full(dve, l, "kk", i)
                for q in range(CH):
                    last = stt(A[:, q, :], bank(l, "kk", i)[:, P * q:P * q + P], beta[:, i, q:q + 1], A[:, q, :],
                               MUL, MUL)
                last.then_inc(free(l, "kk", i), 1)
                wait_full(dve, l, "qk", i)
                tt(QK, v3(bank(l, "qk", i), 4), QK, MUL).then_inc(free(l, "qk", i), 1)
                wait_read(dve, l, "kk", i)
                link(tt(Pm, A, bc(K("m16"), 1, [P, 4, P]), MUL))
                tt(X, bc(ident, 1, [P, 4, P]), Pm, SUB)
                wait_read(dve, l, "at", i)
                link(tt(PT, AT, bc(K("m16t"), 1, [P, 4, P]), MUL))
                tt(XT, bc(ident, 1, [P, 4, P]), PT, SUB).then_inc(sems["x0_ready"], 1)

            def gdn_sq(l, i, q):
                if q == 0:
                    dve.wait_ge(sems["x0_ready"], V("x0_ready", l, i))
                if q < 2:
                    wait_full(dve, l, "sq1", i, q)
                    cp(PT, v3(bank(l, "sq1", i, q), 4)).then_inc(free(l, "sq1", i, q), 1)
                wait_full(dve, l, "xx0", i, q)
                if q:
                    wait_read(dve, l, "xx0", i, q - 1)
                    wait_read(dve, l, "xx1", i, q - 1)
                tt(X, X, v3(bank(l, "xx0", i, q), 4), ADD).then_inc(free(l, "xx0", i, q), 1)
                wait_full(dve, l, "xx1", i, q)
                tt(XT, XT, v3(bank(l, "xx1", i, q), 4), ADD).then_inc(free(l, "xx1", i, q), 1)

            def gdn_lv(l, i, v):
                tt(t1, AT, bc(K(("m32t", "m64t", "m128t")[v]), 1, [P, 4, P]), MUL).then_inc(sems["ot_ready"], 1)
                wait_read(dve, l, *(("xx1", i, 2) if v == 0 else ("lx1", i, v - 1)))
                if v < 2:
                    wait_full(dve, l, "lx0", i, v)
                    wait_full(dve, l, "lx1", i, v)
                    tt(X, X, v3(bank(l, "lx0", i, v), 4), SUB).then_inc(free(l, "lx0", i, v), 1)
                wait_full(dve, l, "lx1", i, v)
                tt(XT, XT, v3(bank(l, "lx1", i, v), 4), SUB).then_inc(free(l, "lx1", i, v), 1)

            def gdn_st(l, i):
                wait_read(dve, l, "vt", i)
                if i:
                    wait_full(dve, l, "ks", i)
                    for q in range(CH):
                        last = stt(R[:, q, :], bank(l, "ks", i)[:, P * q:P * q + P],
                                   nebtok[:, 4 * i + q:4 * i + q + 1], R[:, q, :], MUL, ADD)
                    last.then_inc(free(l, "ks", i), 1)
                    wait_read(dve, l, "ks", i)
                for q in range(CH):
                    last = ts(R[:, q, :], R[:, q, :], beta[:, i, q:q + 1], None, MUL)
                last.then_inc(sems["r_ready"], 1)
                if i:
                    tt(qe, c[:, 0:4, P * i:P * i + P], ebr, MUL).then_inc(sems["qe_ready"], 1)
                wait_read(dve, l, "brow", i)
                tt(dl, blast, btok[:, 4 * i:4 * i + 4], SUB).then_inc(sems["dlx_ready"], 1)
                dve.wait_ge(sems["dl_ready"], V("dl_ready", l, i))
                wait_full(dve, l, "kt", i)
                for q in range(CH):
                    last = ts(kd[:, q, :], bank(l, "kt", i)[:, P * q:P * q + P], dl[:, q:q + 1], None, MUL)
                last.then_inc(free(l, "kt", i), 1)
                wait_full(dve, l, "ds", i)
                if i == 0:
                    cp(S, v3(bank(l, "ds", i), 4)).then_inc(free(l, "ds", i), 1)
                else:
                    wait_read(dve, l, "ds", i - 1)
                    for q in range(CH):
                        last = stt(S[:, q, :], S[:, q, :], ebr[:, q, P - 1:P], bank(l, "ds", i)[:, P * q:P * q + P],
                                   MUL, ADD)
                    last.then_inc(free(l, "ds", i), 1)

            def gdn_s(l):
                def by_bh(t_):
                    return t_.rearrange("p h b -> p b h")

                sb3 = [P, NS, CH]
                v4 = lambda t_: t_.rearrange("p (b h) -> p b h", b=NS)
                cp(v4(s_k), by_bh(c[:, 4:8, NP_TOK:T]))
                tt(v4(s_t), by_bh(c[:, 4:8, NP_TOK:T]), by_bh(c[:, 0:4, NP_TOK:T]), MUL).then_inc(sems["gs_prod"], 1)
                dve.drain().then_inc(sems["gs_k"], 1)
                dve.wait_ge(sems["gs_eg"], V("gs_eg", l))
                d4 = s_d.rearrange("p (n b h) -> p n b h", n=2, b=NS)
                eye = bc(ident[0:NS, 0:NS], 2, [NS, NS, CH])
                tt(d4[:, 0], bc(s_eg[0:NS], 1, [NS, NS, CH]), eye, MUL)
                tt(d4[:, 1], bc(beta[0:NS, 2, :], 1, [NS, NS, CH]), eye, MUL).then_inc(sems["gs_d"], 1)
                wait_full(dve, l, "sgb")
                link(cp(s_bc, bank(l, "sgb")[:, 0:64].rearrange("p (n b h) -> p n b h", n=2, b=NS)))
                dve.drain().then_inc(free(l, "sgb"), 1)
                wait_full(dve, l, "skq")
                kq = bank(l, "skq")[:, 0:64].rearrange("p (b h w) -> p b h w", b=NS, h=CH)
                link(tt(v4(s_u), kq[:, :, :, 1], s_bc[:, 0], MUL))
                link(tt(v4(s_u), by_bh(c[:, 8:12, NP_TOK:T]), v4(s_u), SUB))
                link(tt(v4(s_u), v4(s_u), s_bc[:, 1], MUL))
                link(tt(v4(s_q), kq[:, :, :, 0], s_bc[:, 0], MUL))
                dve.drain().then_inc(free(l, "skq"), 1)
                wait_full(dve, l, "sqk")
                tt(s_t, bank(l, "sqk")[:, 0:32], s_u, MUL).then_inc(free(l, "sqk"), 1)
                wait_read(dve, l, "sqk")
                tt(by_bh(c[:, 8:12, NP_TOK:T]), v4(s_t), v4(s_q), ADD).then_inc(sems["s_o"], 1)
                dve.drain().then_inc(sems["gs_o"], 1)
                tt(S0[:, :, :], S0[:, :, :], bc(s_bc[:, 0].rearrange("p b h -> p (b h)"), 2, [P, 32, CD]), MUL).then_inc(
                    sems["s_state"], 1)
                wait_read(dve, l, "suk")
                for n in range(4):
                    if n >= 2:
                        wait_full(dve, l, "su", 2 * (n - 2) + 1)
                    tt(um[n % 2], bc(uk_sb[:, 0:P], 1, [32, 8, P]), bc(ident[0:32, 8 * n:8 * n + 8], 2, [32, 8, P]),
                       MUL).then_inc(sems["um_ready"], 1)
                    if n == 0:
                        continue
                    add_outer(l, n - 1)
                add_outer(l, 3)
                dve.drain().then_inc(sems["s_new"], 1)

            def add_outer(l, n):
                dve.wait_ge(sems["s_state"], V("s_state", l))
                for m in (2 * n, 2 * n + 1):
                    wait_full(dve, l, "su", m)
                    tt(S0[:, 4 * m:4 * m + 4, :], S0[:, 4 * m:4 * m + 4, :], v3(bank(l, "su", m), 4), ADD).then_inc(
                        free(l, "su", m), 1)

            def gla_la(l):
                dve.wait_ge(sems["bg_sig"], V("bg_sig", l))
                tt(z[:, Z_BG:Z_BG + 4, :], z[:, Z_BG:Z_BG + 4, :], z[:, 8:12, :], MUL)
                for t in range(2):
                    wait_full(dve, l, "la", t)
                    ts(lax[:, t, :], bank(l, "la", t)[:, 0:T], par[:, R_LRB + t:R_LRB + t + 1], None, ADD).then_inc(
                        free(l, "la", t), 1)
                    wait_read(dve, l, "la", t)
                stt(laa[:, :, :], lax[:, :, :], -1.0, lax[:, :, :], MUL, MAX).then_inc(sems["la_x"], 1)
                dve.wait_ge(sems["la_e"], V("la_e", l))
                link(stt(la[:, :, :], lax[:, :, :], 0.0, laa[:, :, :], ALU.min, SUB))
                link(ts(la[:, :, :], la[:, :, :], 1.0 / BTAU, None, MUL))
                for t in range(2):
                    for n in range(4):
                        cols = slice(BC * n, BC * n + BC)
                        last = nc.vector.tensor_tensor_scan(gb[:, t, cols], ones[:, 0:BC], la[:, t, cols], 0.0, MUL, ADD)
                last.then_inc(sems["b_ready"], 1)
                dve.wait_ge(sems["eb_ready"], V("eb_ready", l))
                q4 = qz.rearrange("p (t w) x -> p t w x", w=2)
                for w in range(2):
                    half = slice(64 * w, 64 * w + 64)
                    stt(q4[half, :, w, :], z[half, Z_BQ:Z_BQ + 2, 0:NP_TOK], float(BDK) ** -0.5, geb[half, :, :],
                        MUL, MUL)
                    nc.vector.memset(q4[half, :, 1 - w, :], 0.0)
                tt(keg[:, :, :], z[:, Z_BK:Z_BK + 2, 0:NP_TOK], keg[:, :, :], MUL).then_inc(sems["ke_ready"], 1)

            def gla_at(l, i):
                wait_full(dve, l, "ga", i)
                if i:
                    wait_full(dve, l, "go", i - 1)
                tt(gatt, v3(bank(l, "ga", i), 4), bc(K("gla"), 1, [P, BH, P]), MUL).then_inc(free(l, "ga", i), 1)

            def gla_ch(l, n):
                if n:
                    wait_read(dve, l, "go", n // 2)
                    wait_full(dve, l, "gi", n)
                    o_ = ob[:, :, BC * n:BC * n + BC]
                    tt(o_, o_, v3(bank(l, "gi", n)[:, 0:256], 4), ADD).then_inc(free(l, "gi", n), 1)
                wait_full(dve, l, "gs", n)
                d_ = v3(bank(l, "gs", n)[:, 0:256], 2)
                if n == 0:
                    cp(GS, d_).then_inc(free(l, "gs", n), 1)
                else:
                    dve.wait_ge(sems["gla_state"], V("gla_state", l, n - 1))
                    tt(GS, GS, d_, ADD).then_inc(free(l, "gs", n), 1)
                wait_read(dve, l, "gs", n)
                tt(GS, GS, geb[:, :, BC * n + BC - 1:BC * n + BC].to_broadcast([P, 2, BDV]), MUL).then_inc(
                    sems["gla_state"], 1)

            def gla_s(l):
                wait_read(dve, l, "gv")
                dve.wait_ge(gs0_in, 32 * (l + 1))
                link(tt(g_s0.rearrange("p q b v -> p (q b) v"), g_s0.rearrange("p q b v -> p (q b) v"),
                        bc(g_a, 2, [P, 16, BDV]), MUL))
                for n in range(4):
                    if n >= 2:
                        wait_full(dve, l, "gu", 1)
                    tt(vm[n % 2], bc(g_v[:, P * n:P * n + P], 1, [NS, NS, P]), bc(ident[0:NS, 0:NS], 2, [NS, NS, P]),
                       MUL).then_inc(sems["vm_ready"], 1)
                    if n % 2:
                        for m in (n - 1, n):
                            wait_full(dve, l, "gu", m)
                            s_ = g_s0[:, m // 2, 4 * (m % 2):4 * (m % 2) + 4, :]
                            tt(s_, s_, v3(bank(l, "gu", m), 4), ADD).then_inc(free(l, "gu", m), 1)
                o4 = ob.rearrange("p (t w) x -> p t w x", w=2)
                for w in range(2):
                    wait_full(dve, l, "gq", w)
                    ts(o4[:, :, w, NP_TOK:T], v3(bank(l, "gq", w)[:, 0:16], 2), float(BDK) ** -0.5, None, MUL).then_inc(
                        free(l, "gq", w), 1)

            def kv_tok(l):
                m = 0
                for i in range(TT):
                    for g in range(NG):
                        if m >= 2:
                            wait_read(dve, l, "tk", (m - 2) // NG, (m - 2) % NG)
                            done = K_STORES[m % 2] * l + (m - 2 + m % 2) // 2
                            if done:
                                dve.wait_ge(stored[f"k{m % 2}"], 16 * done)
                        wait_full(dve, l, "tk", i, g)
                        cp(kst[m % 2], bank(l, "tk", i, g)).then_inc(free(l, "tk", i, g), 1)
                        m += 1

            def att(l, q):
                bt = btab[q % 2]
                dve.wait_ge(tab_in[q % 2], 16 * (4 * l + q // 2 + 1))
                for i in range(TT):
                    u, w = 2 * q + i, P * (i + 1)
                    wait_full(dve, l, "sc", q, i, 0)
                    s3 = v3(sc[i][:, 0:NG * w], NG)
                    g_ = NG - i
                    tt(s3[:, 0:g_, :], v3(bank(l, "sc", q, i, 0)[:, 0:g_ * w], g_), bt[:, 0:g_, 256 - w:256],
                       ADD).then_inc(free(l, "sc", q, i, 0), 1)
                    if i:
                        wait_full(dve, l, "sc", q, i, 1)
                        tt(s3[:, 2, :], bank(l, "sc", q, i, 1)[:, 0:w], bt[:, 2, :], ADD).then_inc(
                            free(l, "sc", q, i, 1), 1)
                        wait_read(dve, l, "sc", q, i, 1)
                    wait_read(dve, l, "sc", q, i, 0)
                    nc.vector.tensor_reduce(rowmax[:, u:u + 1], sc[i][:, 0:NG * w], AX.X, MAX, negate=True).then_inc(
                        sems["sc_add"], 1)
                    dve.wait_ge(sems["p_ready"], V("p_ready", l, u))
                    link(nc.vector.reciprocal(rowinv[:, u:u + 1], rowsum[:, u:u + 1]))
                    wait_full(dve, l, "pv", q, i)
                    ts(oat[:, i, DH * q:DH * q + DH], bank(l, "pv", q, i)[:, 0:DH], rowinv[:, u:u + 1], None,
                       MUL).then_inc(free(l, "pv", q, i), 1)

            def att_s(l):
                for n in range(6):
                    wait_read(dve, l, "ts", n)
                for g in range(NG):
                    link(tt(prod[0][0:NS, :], tok_g[:, 0, g, :], tok_g[:, 1, g, :], MUL))
                    link(nc.vector.tensor_reduce(sself[:, 8 * g:8 * g + 8], v3(prod[0][0:NS, :], AH), AX.X, ADD))
                tt(sself, sself, bself, ADD).then_inc(sems["ls_ready"], 1)
                for n in range(NG * NS):
                    g, b = n // NS, n % NS
                    dve.wait_ge(cache_in[n % 6], 16 * (8 * l + n // 6 + 1))
                    wait_full(dve, l, "qb", n)
                    tt(prod[n % 2], cache[n % 6], bank(l, "qb", n), MUL).then_inc(free(l, "qb", n), 1)
                    wait_read(dve, l, "qb", n)
                    last = nc.vector.tensor_reduce(L[:, 64 * g + 8 * b:64 * g + 8 * b + 8], v3(prod[n % 2], AH), AX.X, ADD)
                link(last)
                l4 = L.rearrange("p (g b h) -> p g b h", g=NG, b=NS)
                tt(l4, l4, bc(v3(biask, NG), 2, [P, NG, NS, AH]), ADD).then_inc(sems["l_ready"], 1)
                wait_full(dve, l, "sx")
                tt(sself2, bank(l, "sx")[0:64, 0:24], K("hsel", 64), MUL).then_inc(free(l, "sx"), 1)
                wait_read(dve, l, "sx")
                link(nc.vector.tensor_reduce(sp_[:, NG * P:NG * P + NG], v3(sself2, NG), AX.X, ADD))
                wait_full(dve, l, "lt")
                cp(sp_[:, 0:NG * P], bank(l, "lt")[0:64, 0:NG * P]).then_inc(free(l, "lt"), 1)
                wait_read(dve, l, "lt")
                nc.vector.tensor_reduce(rowmax[0:64, 0:1], sp_, AX.X, MAX, negate=True).then_inc(sems["sp_max"], 1)
                dve.wait_ge(sems["ps_ready"], V("ps_ready", l))
                link(nc.vector.reciprocal(rowinv[0:64, 0:1], rowsum[0:64, 0:1]))
                for g in range(NG):
                    ts(dd[:, g, :], K("bsel", 64), sp_[:, NG * P + g:NG * P + g + 1], None, MUL)
                ts(dd[:, 3, :], K("bsel", 64), rowinv[0:64, 0:1], None, MUL).then_inc(sems["dd_ready"], 1)
                wait_full(dve, l, "rr")
                cp(rrs, bank(l, "rr")[:, 0:P]).then_inc(free(l, "rr"), 1)
                wait_read(dve, l, "rr")
                r4 = rrs.rearrange("p (t n b) -> p t n b", t=4, n=4)
                o_, v_ = oaT[:, :, NP_TOK:T], v3(vprod, 4)
                wait_full(dve, l, "pvs")
                link(cp(o_, v3(bank(l, "pvs")[:, 0:32], 4)))
                dve.drain().then_inc(free(l, "pvs"), 1)
                for g in range(NG):
                    link(tt(v_, z[:, Z_V + 4 * g:Z_V + 4 * g + 4, NP_TOK:T], r4[:, :, g, :], MUL))
                    link(tt(o_, o_, v_, ADD))
                tt(o_, o_, r4[:, :, 3, :], MUL).then_inc(sems["oas_ready"], 1)

            def bar(l, n):
                dve.wait_ge(sems["bar_a"], V("bar_a", l, n))
                dve.wait_ge(sems["bar_p"], V("bar_p", l, n))
                dve.drain().then_inc(sems["bar_v"], 1)
                dve.wait_ge(sems["bar_v"], V("bar_v", l, n))

            def merge(l):
                dve.wait_ge(sems["sig_ready"], V("sig_ready", l))
                for b in range(3):
                    for d in range(KT):
                        wait_full(dve, l, "mb", b, d)
                        g_ = z[:, Z_G + 8 * b + d, :]
                        if b == 0:
                            tt(z[:, d, :], bank(l, "mb", b, d)[:, 0:T], g_, MUL).then_inc(free(l, "mb", b, d), 1)
                            continue
                        tt(z[:, 8 + d % 4, :], bank(l, "mb", b, d)[:, 0:T], g_, MUL).then_inc(free(l, "mb", b, d), 1)
                        wait_read(dve, l, "mb", b, d)
                        wait_read(dve, l, "mb", 0, d)
                        if b == 1:
                            steps[0] += 1
                            tt(z[:, d, :], z[:, d, :], z[:, 8 + d % 4, :], ADD).then_inc(vec, 1)
                        else:
                            dve.wait_ge(vec, steps[0])
                            last = tt(z[:, d, :], z[:, d, :], z[:, 8 + d % 4, :], ADD)
                last.then_inc(sems["acc_ready"], 1)
                for d in range(KT):
                    wait_full(dve, l, "wo", d)
                    tt(x[:, d, :], x[:, d, :], bank(l, "wo", d)[:, 0:T], ADD).then_inc(free(l, "wo", d), 1)

            def ffn0():
                for i in range(FF // P):
                    wait_read(dve, 0, "fg", i)
                    wait_full(dve, 0, "fu", i)
                    tt(fa[:, i, :], fs[:, i % 4, :], bank(0, "fu", i)[:, 0:T], MUL).then_inc(free(0, "fu", i), 1)
                for d in range(KT):
                    wait_full(dve, 0, "fd", d)
                    tt(x[:, d, :], x[:, d, :], bank(0, "fd", d)[:, 0:T], ADD).then_inc(free(0, "fd", d), 1)

            def route():
                r3 = [P, 3, NE]
                wait_full(dve, 1, "rl", 0)
                cp(rlog[0:NE, :], bank(1, "rl", 0)[0:NE, 0:T]).then_inc(free(1, "rl", 0), 1)
                link(nc.vector.memset(rl, 0.0))
                wait_full(dve, 1, "rt", 0)
                cp(rl[:, 0:2, :], v3(bank(1, "rt", 0)[:, 0:16], 2))
                cp(rl[0:NS, 2, :], bank(1, "rt", 0)[0:NS, 16:24]).then_inc(free(1, "rt", 0), 1)
                wait_read(dve, 1, "rt", 0)

                def top(src, m, first):
                    link(nc.vector.tensor_reduce(m, src, AX.X, MAX))
                    link(tt(req, src, bc(m, 2, r3), ALU.is_equal))
                    for i in range(3):
                        last = nc.vector.tensor_tensor_scan(rcum[:, i, :], ones[:, 0:NE], req[:, i, :], 0.0, MUL, ADD)
                    link(last)
                    link(stt(first, rcum, 1.0, req, ALU.is_equal, MUL))

                top(rl, rm1, rf1)
                link(stt(rl2, rf1, NEG, rl, MUL, ADD))
                top(rl2, rm2, rf2)
                tt(rexp, rm2, rm1, SUB).then_inc(r_max, 1)
                dve.wait_ge(r_exp, 1)
                link(ts(rden, rexp, 1.0, None, ADD))
                link(nc.vector.reciprocal(rden, rden))
                link(tt(rexp, rexp, rden, MUL))
                tt(rmask, rf1, rf2, ADD).then_inc(r_mask, 1)
                link(tt(rf1, rf1, bc(rden, 2, r3), MUL))
                link(tt(rf2, rf2, bc(rexp, 2, r3), MUL))
                tt(rg, rf1, rf2, ADD).then_inc(r_gate, 1)
                wait_full(dve, 1, "gt", 0)
                cp(gT[0:NE, :], bank(1, "gt", 0)[0:NE, 0:T]).then_inc(free(1, "gt", 0), 1)
                wait_read(dve, 1, "gt", 0)
                tt(g8, bc(gT[0:NE, :], 1, [NE, NE, T]), bc(ident[0:NE, 0:NE], 2, [NE, NE, T]), MUL).then_inc(r_gate, 1)
                wait_full(dve, 1, "rp", 0)
                b_ = bank(1, "rp", 0)
                link(nc.vector.memset(rpos, 0.0))
                ts(rpos[:, 0:2, :], v3(b_[:, 0:16], 2), -1.0, None, ADD)
                ts(rpos[0:NS, 2, :], b_[0:NS, 16:24], -1.0, None, ADD)
                nc.vector.tensor_reduce(rmost, b_[:, 24:32], AX.X, MAX).then_inc(free(1, "rp", 0), 1)
                wait_read(dve, 1, "rp", 0)
                ts(crowded[0:1, 0:1], rmost[0:1, :], float(P) + 0.5, None, ALU.is_gt).then_inc(r_flag, 1)
                for e in range(NE):
                    if e >= 2:
                        wait_full(dve, 1, "st", e - 2)
                    for i, (_, nt) in enumerate(TOKS):
                        at_ = rpos[0:nt, i, e:e + 1]
                        slots = ts(G[0:nt, i, e, :], K("iota")[0:nt, :], at_, rmask[0:nt, i, e:e + 1], ALU.is_equal, MUL)
                        if e == NE - 1 and i == 2:
                            slots.then_inc(r_slots, 1)
                        last = ts(gw[e % 2][0:nt, i, :], K("iota")[0:nt, :], at_, rg[0:nt, i, e:e + 1], ALU.is_equal, MUL)
                    last.then_inc(r_back, 1)

            def experts_all():
                with dve.Fori(0, NE) as e:
                    wait_full(dve, 1, "gh", 0, e=e)
                    cp(gB[:, 0, :], bank(1, "gh", 0)[:, 0:T]).then_inc(free(1, "gh", 0), 1)
                    wait_full(dve, 1, "gh", 1, e=e)
                    cp(gB[:, 1, 0:8], bank(1, "gh", 1)[:, 0:8]).then_inc(free(1, "gh", 1), 1)
                    wait_read(dve, 1, "gh", 0, e=e)
                    wait_read(dve, 1, "gh", 1, e=e)
                    for i in range(FE // P):
                        wait_read(dve, 1, "fg", i, e=e)
                        tt(ft[:, i % 4, :], fs[:, i % 4, :], gB[:, 0, :], MUL).then_inc(silu_used, 1)
                        wait_full(dve, 1, "fu", i, e=e)
                        dve.wait_ge(silu_used, e * (FE // P) + (1 + i))
                        tt(fa[:, i, :], ft[:, i % 4, :], bank(1, "fu", i)[:, 0:T], MUL).then_inc(free(1, "fu", i), 1)
                    add_x(e)

            def add_x(e):
                for d in range(KT):
                    wait_full(dve, 1, "fd", d, e=e)
                    tt(x[:, d, :], x[:, d, :], bank(1, "fd", d)[:, 0:T], ADD).then_inc(free(1, "fd", d), 1)

            def experts_chosen():
                with dve.Fori(0, NE) as e:
                    for i in range(FE // P):
                        wait_read(dve, 1, "fg", i, e=e)
                        wait_full(dve, 1, "fu", i, e=e)
                        tt(fa[:, i, 0:P], fs[:, i % 4, 0:P], bank(1, "fu", i)[:, 0:P], MUL).then_inc(
                            free(1, "fu", i), 1)
                    add_x(e)

            def experts():
                dve.wait_ge(r_flag, 1)
                many = dve.value_load(crowded[0:1, 0:1], min_val=0, max_val=1)
                with dve.If(many):
                    experts_all()
                with dve.Else():
                    experts_chosen()

            nc.vector.memset(relb[NB:NB + 1, :], 1.0).then_inc(relb_one, 1)
            link(nc.vector.memset(cba, 0.0))
            run = dict(small=small_step, conv=conv, gate_c=gate_c, norm4=norm4, gdn_dec=gdn_dec, gdn_a=gdn_a,
                       gdn_sq=gdn_sq, gdn_lv=gdn_lv, gdn_st=gdn_st, gdn_s=gdn_s, gla_la=gla_la,
                       gla_at=gla_at, gla_ch=gla_ch, gla_s=gla_s, kv_tok=kv_tok, att=att, att_s=att_s,
                       merge=merge, xnorm=xnorm,
                       bar=bar)
            for l in range(DEPTH):
                for step in SCHED[l]:
                    if step[0] in run:
                        if step[0] != "proj":
                            settle()
                        run[step[0]](l, *step[1:])
                settle()
                xnorm(l, 1)
                if l == 0:
                    ffn0()
                else:
                    route()
                    experts()

        @block.gpsimd
        def _(pool):
            def load_params(l):
                def row(r, n, src):
                    pool.dma_start(prow[r:r + n, :], src).then_inc(prow_in, 16)

                row(R_NM, KT, a["norm_mix"][l].rearrange("(k p) -> k p", p=P))
                row(R_NF, KT, a["norm_ffn"][l].rearrange("(k p) -> k p", p=P))
                row(R_LRB, 2, a["b_lr_bias"][l].rearrange("(k p) -> k p", p=P))
                row(R_BO, 1, a["b_out_norm"][l:l + 1, :])
                row(R_CO, 1, a["c_out_norm"][l:l + 1, :])
                row(R_CV, 48, a["c_conv"][l].rearrange("w (k p) -> (w k) p", p=P))
                for n in range(2):
                    for r, name in ((R_QN, "a_q_norm"), (R_KN, "a_k_norm")):
                        pool.dma_start(prow[r:r + 1, DH * n:DH * n + DH], a[name][l:l + 1, :]).then_inc(prow_in, 16)
                pool.dma_start(arow[:, 0:4], a["c_a_log"][l:l + 1, :]).then_inc(prow_in, 16)
                pool.dma_start(arow[:, 4:8], a["c_dt_bias"][l:l + 1, :]).then_inc(prow_in, 16)

            def load_small_w(l):
                w = a["w_in"][l].rearrange("(k p) n -> p k n", p=P)
                pool.dma_start(wsm[:, :, 0:BRANK], w[:, :, 6144:6160]).then_inc(wsm_in, 16)
                pool.dma_start(wsm[:, :, BRANK:24], w[:, :, 8208:8216]).then_inc(wsm_in, 16)

            def load_conv(l):
                pool.dma_start(convt, a["state_conv"][l].rearrange("b j n -> (b j) n")).then_inc(convt_in, 16)

            def conv(l):
                for q in range(3):
                    wait_read(pool, l, "co", q)
                pool.dma_start(o["conv_p"][l, 0], convt[0:3, :]).then_inc(stored["conv"], 16)
                pool.dma_start(o["conv_s"][l, :, 2, :], convt[3:11, :]).then_inc(stored["conv"], 16)
                pool.dma_start(o["conv_s"][l, :, 0:2, :], a["state_conv"][l, :, 1:3, :]).then_inc(stored["conv"], 16)

            def gdn_s(l):
                wait_read(pool, l, "ds", 1)
                pool.dma_start(S0, a["state_gdn"][l].rearrange("b h d v -> d (b h) v")).then_inc(s0_in, 16)
                pool.dma_start(o["gdn_p"][l, 0].rearrange("h d v -> d h v"), S).then_inc(stored["gdn"], 16)
                pool.wait_ge(sems["s_new"], V("s_new", l))
                pool.dma_start(o["gdn_s"][l].rearrange("b h d v -> d (b h) v"), S0).then_inc(stored["gdns"], 16)
                pool.wait_ge(stored["gdn"], 16 * (l + 1))
                pool.wait_ge(stored["gdns"], 16 * (l + 1))

            def gla_la(l):
                for q in range(2):
                    pool.dma_start(g_s0[:, q], a["state_gla"][l].rearrange(
                        "b (q w) d v -> q (w d) b v", q=2)[q]).then_inc(gs0_in, 16)

            def gla_s(l):
                pool.wait_ge(sems["gla_state"], V("gla_state", l, 3))
                pool.dma_start(o["gla_p"][l, 0].rearrange("(q w) d v -> (w d) q v", q=2), GS).then_inc(stored["gla"], 16)
                for m in range(4):
                    wait_read(pool, l, "gu", m)
                for q in range(2):
                    pool.dma_start(o["gla_s"][l].rearrange("b (q w) d v -> q (w d) b v", q=2)[q],
                                   g_s0[:, q]).then_inc(stored["glas"], 16)
                pool.wait_ge(stored["gla"], 16 * (l + 1))
                pool.wait_ge(stored["glas"], 32 * (l + 1))
                if l == 0:
                    pool.dma_start(wlr, a["b_w_lr"][1]).then_inc(wlr_in, 16)

            def bias_tables(l, q):
                if q >= 2:
                    wait_read(pool, l, "sc", q - 2, 1, 0)
                    wait_read(pool, l, "sc", q - 2, 1, 1)
                src = bass.AP(tensor=dscr.tensor, offset=q * P * 512, ap=[[511, P], [AH * P * 512, NG], [1, 256]])
                pool.dma_start(btab[q % 2], src).then_inc(tab_in[q % 2], 16)

            def kv_tok(l):
                pool.wait_ge(tab_out[0], 16)
                bias_tables(l, 0)
                bias_tables(l, 1)
                m = 0
                for i in range(TT):
                    for g, (win, _) in enumerate(GROUPS):
                        r0 = 0 if win == P else P * i
                        dst = o[f"win{win}_p"][l, 0, r0:r0 + P]
                        wait_read(pool, l, "tk", i, g)
                        if win > P or i:
                            pool.dma_start(dst[:, 0].rearrange("t h d -> t (h d)"), kst[m % 2]).then_inc(
                                stored[f"k{m % 2}"], 16)
                            wait_read(pool, l, "tk", i, 3 + g)
                            pool.dma_start(dst[:, 1].rearrange("t h d -> t (h d)"),
                                           vtok[:, i, 512 * g:512 * g + 512]).then_inc(stored["v"], 16)
                        m += 1

            def att(l, q):
                if q >= 2:
                    bias_tables(l, q)
                if q == AH - 1:
                    for n in ("k0", "k1", "v"):
                        pool.wait_ge(stored[n], 16 * STORES[n] // DEPTH * (l + 1))

            def load_cache(l, n):
                m = n - 24
                g, b, kv = (n // NS, n % NS, 0) if n < 24 else (m % NG, m // NG, 1)
                if n >= 30:
                    pool.wait_ge(sems["v_used"], 7 * l + (n - 30) // NG + 1)
                elif n >= 6:
                    wait_read(pool, l, "qb", n - 6)
                name, win = CACHES[g]
                src = a[name][l, b].rearrange("(w s) k h d -> w s k (h d)", s=win // P)[:, 0, kv]
                pool.dma_start(cache[n % 6], src).then_inc(cache_in[n % 6], 16)

            def att_s(l):
                for n in range(48):
                    load_cache(l, n)
                    if n == 12:
                        for g, (win, _) in enumerate(GROUPS):
                            for kv in range(2):
                                wait_read(pool, l, "ts", 3 * (1 + kv) + g)
                                pool.dma_start(o[f"win{win}_s"][l, :, win - 1, kv].rearrange("b h d -> b (h d)"),
                                               tok_g[:, 1 + kv, g, :]).then_inc(stored["toks"], 16)

            def bar(l, n):
                if n == 4:
                    pool.wait_ge(stored["toks"], 96 * (l + 1))
                    pool.wait_ge(sems["oas_ready"], V("oas_ready", l))
                pool.drain().then_inc(sems["bar_p"], 1)
                pool.wait_ge(sems["bar_v"], V("bar_v", l, n))
                if l == 0 and n == 0:
                    wait_read(pool, 0, "par")
                    wait_full(pool, 0, "ab")
                    load_params(1)
                    wait_full(pool, 0, "lr")
                    load_small_w(1)
                if l == 0 and n == 4:
                    pool.wait_ge(stored["conv"], 48)
                    load_conv(1)

            pool.dma_start(setup, a["const_setup"]).then_inc(setup_in, 16)
            pool.dma_start(relb[0:NB, :], a["rel_bias"]).then_inc(relb_in, 16)
            load_params(0)
            load_small_w(0)
            load_conv(0)
            pool.dma_start(wlr, a["b_w_lr"][0]).then_inc(wlr_in, 16)
            run = dict(conv=conv, gdn_s=gdn_s, gla_la=gla_la, gla_s=gla_s, kv_tok=kv_tok, att=att, att_s=att_s, bar=bar)
            for l in range(DEPTH):
                for step in SCHED[l]:
                    if step[0] in run:
                        run[step[0]](l, *step[1:])
            pool.dma_start(v3(wr, KT), a["moe_router"][0].rearrange("(k p) n -> p k n", p=P)).then_inc(router_in, 16)


CACHES = (("cache_win128_kv", 128), ("cache_win512_kv", 512), ("cache_win2048_kv", 2048))
STORES = dict(k0=4, k1=6, v=10, conv=6, gdn=2, gdns=2, gla=2, glas=4, toks=12, copy=48, y=3)
K_STORES = (2, 3)

_INS = ["x_prompt", "x_sample", "cache_win128_kv", "cache_win512_kv", "cache_win2048_kv", "state_gla", "state_gdn",
        "state_conv", "norm_mix", "w_in", "a_q_norm", "a_k_norm", "rel_bias", "b_w_lr", "b_lr_bias", "b_out_norm",
        "c_conv", "c_a_log", "c_dt_bias", "c_out_norm", "w_branch", "w_out", "norm_ffn", "ffn_w_gate", "ffn_w_up",
        "ffn_w_down", "moe_router", "moe_w_gate", "moe_w_up", "moe_w_down"]


def _win(batch, n):
    return (DEPTH, batch, n, 2, AH, DH)


_OUTS = [("y_prompt", (1, NP_TOK, D)), ("y_sample", (NS, 1, D)),
         ("win128_p", _win(1, 128)), ("win128_s", _win(NS, 128)),
         ("win512_p", _win(1, NP_TOK)), ("win512_s", _win(NS, 512)),
         ("win2048_p", _win(1, NP_TOK)), ("win2048_s", _win(NS, 2048)),
         ("gla_p", (DEPTH, 1, BH, BDK, BDV)), ("gla_s", (DEPTH, NS, BH, BDK, BDV)),
         ("gdn_p", (DEPTH, 1, CH, CD, CD)), ("gdn_s", (DEPTH, NS, CH, CD, CD)),
         ("conv_p", (DEPTH, 1, CONVW - 1, CCH)), ("conv_s", (DEPTH, NS, CONVW - 1, CCH))]


def kernel(**inputs):
    import numpy as _np
    import concourse.bacc as _bacc
    from concourse.bass_utils import run_bass_kernel_spmd as _run

    nc = _bacc.Bacc("TRN2", target_bir_lowering=False, num_devices=1)
    arrays, ins, outs = {}, {}, {}
    main, setup = constants()
    for name, arr in [(n, _np.ascontiguousarray(inputs[n])) for n in _INS] + [("const_main", main),
                                                                              ("const_setup", setup)]:
        arrays[f"in_{name}"] = arr
        ins[name] = nc.dram_tensor(f"in_{name}", arr.shape, F32, kind="ExternalInput").ap()
    for name, shape in _OUTS:
        outs[name] = nc.dram_tensor(f"out_{name}", shape, F32, kind="ExternalOutput").ap()
    build(nc, ins, outs)
    r = _run(nc, [arrays], core_ids=[0])
    return tuple(r.results[0][f"out_{name}"] for name, _ in _OUTS)
```
